# Optimizing a Trainium2 kernel written in Bass

```python
import math
import jax, jax.numpy as jnp
from jax import lax
import numpy as np

D_MODEL = 1024
BATCH = 1
SEQ = 1024
DEPTH = 1
DEC_BATCH = 8
DEC_SEQ = 1
PAST_LEN = 2048
PAGE_SIZE = 128

RW_HEADS = 8
RW_HEAD = 64
RW_WIDTH = RW_HEADS * RW_HEAD
DECAY_LORA = 64
AAA_LORA = 64
GATE_LORA = 128
RW_COLS = 3 * RW_WIDTH + DECAY_LORA + AAA_LORA + GATE_LORA
RW_GN_EPS = 1e-5 * RW_HEAD * RW_HEAD
DA_HEADS = 4
DA_QK = 64
DA_V = 2 * DA_QK
DA_QK_WIDTH = 2 * DA_HEADS * DA_QK
DA_V_WIDTH = DA_HEADS * DA_V
DA_COLS = 2 * DA_QK_WIDTH + DA_V_WIDTH
GATE_COLS = 2 * D_MODEL
IN_COLS = RW_COLS + DA_COLS + GATE_COLS
D_FF = 128 * ((8 * D_MODEL // 3 + 127) // 128)
ROPE_THETA = 10000.0
Q_BLOCK = 128
NORM_EPS = 1e-6
F32 = jnp.float32

kernel_name = "rwkv7_diffattn_macaron_hybrid_step"

def rms_norm(x, g):
    xf = x.astype(F32)
    y = xf * lax.rsqrt(jnp.mean(jnp.square(xf), axis=-1, keepdims=True) + NORM_EPS)
    return (y * g.astype(F32)).astype(x.dtype)

def swiglu(x, w_up, w_down):
    gate, up = jnp.split(x @ w_up, 2, axis=-1)
    return (jax.nn.silu(gate) * up) @ w_down

def rope(x, pos):
    half = x.shape[-1] // 2
    inv = ROPE_THETA ** (-jnp.arange(half, dtype=F32) / half)
    ang = pos.astype(F32)[:, None] * inv[None, :]
    cos = jnp.cos(ang)[:, None, :]
    sin = jnp.sin(ang)[:, None, :]
    xf = x.astype(F32)
    x1, x2 = xf[..., :half], xf[..., half:]
    return jnp.concatenate([x1 * cos - x2 * sin, x2 * cos + x1 * sin], axis=-1).astype(x.dtype)

def diff_attn_core(q, k, v, q_pos, k_pos, lam):
    b, tq = q.shape[:2]
    tk = k.shape[1]
    s = jnp.einsum("bqhd,bkhd->bhqk", q, k).astype(F32) * (DA_QK ** -0.5)
    s = jnp.where(k_pos[None, :] <= q_pos[:, None], s, -jnp.inf)
    p = jax.nn.softmax(s, axis=-1).reshape(b, DA_HEADS, 2, tq, tk)
    w = p[:, :, 0] - lam * p[:, :, 1]
    return jnp.einsum("bhqk,bkhd->bqhd", w.astype(v.dtype), v)

def diff_attn_prompt(q, k, v, lam):
    b, s = q.shape[:2]
    nb = s // Q_BLOCK
    pos = jnp.arange(s, dtype=jnp.int32)
    qb = q.reshape(b, nb, Q_BLOCK, 2 * DA_HEADS, DA_QK).swapaxes(0, 1)
    pb = pos.reshape(nb, Q_BLOCK)
    out = lax.map(lambda a: diff_attn_core(a[0], k, v, a[1], pos, lam), (qb, pb))
    return out.swapaxes(0, 1).reshape(b, s, DA_HEADS, DA_V)

def diff_attn_sample(q, k_new, v_new, cache_k, cache_v, page_table, lam):
    t = q.shape[1]
    n_past = page_table.shape[1] * PAGE_SIZE
    q_pos = n_past + jnp.arange(t, dtype=jnp.int32)
    k_pos = jnp.arange(n_past + t, dtype=jnp.int32)

    def one(args):
        qi, ki, vi, pt = args
        kp = cache_k[pt].reshape(n_past, 2 * DA_HEADS, DA_QK)
        vp = cache_v[pt].reshape(n_past, DA_HEADS, DA_V)
        kk = jnp.concatenate([kp, ki.astype(kp.dtype)], axis=0)
        vv = jnp.concatenate([vp, vi.astype(vp.dtype)], axis=0)
        return diff_attn_core(qi[None], kk[None], vv[None], q_pos, k_pos, lam)[0].astype(qi.dtype)

    return lax.map(one, (q, k_new, v_new, page_table))

def wkv7_scan(state0, r, w, k, v, a, b):
    def step(S, inp):
        r_t, w_t, k_t, v_t, a_t, b_t = inp
        Sa = jnp.einsum("bhij,bhj->bhi", S, a_t)
        S = S * w_t[:, :, None, :] + Sa[..., None] * b_t[:, :, None, :] + v_t[..., None] * k_t[:, :, None, :]
        return S, jnp.einsum("bhij,bhj->bhi", S, r_t)

    xs = tuple(t.swapaxes(0, 1) for t in (r, w, k, v, a, b))
    S, ys = lax.scan(step, state0, xs)
    return ys.swapaxes(0, 1), S

def rwkv7_branch(z, z_last, wkv0, lp):
    bsz, t, _ = z.shape
    z_prev = jnp.concatenate([z_last[:, None, :].astype(z.dtype), z[:, :-1]], axis=1)
    zm = z + (z_prev - z) * lp["rw_mu"]
    o1 = RW_WIDTH
    o4 = 3 * RW_WIDTH + DECAY_LORA
    r, k, v, wd, ad, gd = jnp.split(zm, [o1, 2 * o1, 3 * o1, o4, o4 + AAA_LORA], axis=-1)
    w_log = -jax.nn.softplus(-(lp["rw_w0"] + jnp.tanh(wd) @ lp["rw_w2"]).astype(F32)) - 0.5
    decay = jnp.exp(-jnp.exp(w_log))
    a = jax.nn.sigmoid(lp["rw_a0"] + ad @ lp["rw_a2"])
    g = jax.nn.sigmoid(gd) @ lp["rw_g2"]
    heads = lambda u: u.reshape(bsz, t, RW_HEADS, RW_HEAD).astype(F32)
    kk = heads(k * lp["rw_k_k"])
    kk = kk / jnp.maximum(jnp.linalg.norm(kk, axis=-1, keepdims=True), 1e-12)
    k = k * (1.0 + (a - 1.0) * lp["rw_k_a"])
    rh, kh, vh, ah = heads(r), heads(k), heads(v), heads(a)
    y, wkv = wkv7_scan(wkv0.astype(F32), rh, heads(decay), kh, vh, -kk, kk * ah)
    mu = jnp.mean(y, axis=-1, keepdims=True)
    var = jnp.mean(jnp.square(y - mu), axis=-1, keepdims=True)
    y = (y - mu) * lax.rsqrt(var + RW_GN_EPS)
    y = y * lp["rw_ln_w"].astype(F32).reshape(RW_HEADS, RW_HEAD) + lp["rw_ln_b"].astype(F32).reshape(RW_HEADS, RW_HEAD)
    y = y + jnp.sum(rh * kh * lp["rw_r_k"].astype(F32), axis=-1, keepdims=True) * vh
    y = y.reshape(bsz, t, RW_WIDTH).astype(z.dtype) * g
    return y, wkv.astype(wkv0.dtype), z[:, -1]

def decoder_layer(x, pos, wkv0, z_last, attend, lp, lam_init):
    bsz, t, _ = x.shape
    x = x + 0.5 * swiglu(rms_norm(x, lp["ffn1_norm"]), lp["ffn1_up"], lp["ffn1_down"])
    h = rms_norm(x, lp["mix_norm"])
    proj = h @ lp["w_in"]
    z_rw, q, k, v, gates = jnp.split(
        proj, [RW_COLS, RW_COLS + DA_QK_WIDTH, RW_COLS + 2 * DA_QK_WIDTH, RW_COLS + DA_COLS], axis=-1)
    y_a, wkv, z_new = rwkv7_branch(z_rw, z_last, wkv0, lp)
    q = rope(q.reshape(bsz, t, 2 * DA_HEADS, DA_QK), pos)
    k = rope(k.reshape(bsz, t, 2 * DA_HEADS, DA_QK), pos)
    v = v.reshape(bsz, t, DA_HEADS, DA_V)
    o = attend(q, k, v)
    o = rms_norm(o, lp["da_subln"].reshape(DA_HEADS, DA_V)) * (1.0 - lam_init)
    y_b = o.reshape(bsz, t, DA_V_WIDTH)
    g_a, g_b = jnp.split(jax.nn.sigmoid(gates + lp["gate_bias"]), 2, axis=-1)
    merged = g_a * (y_a @ lp["w_proj_a"]) + g_b * (y_b @ lp["w_proj_b"])
    x = x + merged @ lp["w_out"]
    x = x + 0.5 * swiglu(rms_norm(x, lp["ffn2_norm"]), lp["ffn2_up"], lp["ffn2_down"])
    return x, k, v, wkv, z_new

def setup_inputs(seed: int = 0) -> dict:
    key = jax.random.key(seed)
    ks = iter(jax.random.split(key, 64))
    nrm = lambda shape, s=1.0: jax.random.normal(next(ks), shape, F32) * s
    L = DEPTH
    n_pages = PAST_LEN // PAGE_SIZE
    n_phys = (DEC_BATCH * n_pages * 5) // 4
    perm = jax.random.permutation(next(ks), n_phys)
    page_table = perm[: DEC_BATCH * n_pages].reshape(DEC_BATCH, n_pages).astype(jnp.int32)
    return {
        "x_prompt": nrm((BATCH, SEQ, D_MODEL)),
        "x_sample": nrm((DEC_BATCH, DEC_SEQ, D_MODEL)),
        "cache_k": nrm((L, n_phys, PAGE_SIZE, 2 * DA_HEADS, DA_QK)),
        "cache_v": nrm((L, n_phys, PAGE_SIZE, DA_HEADS, DA_V)),
        "state_wkv": nrm((L, DEC_BATCH, RW_HEADS, RW_HEAD, RW_HEAD), 0.5),
        "state_shift": nrm((L, DEC_BATCH, RW_COLS)),
        "page_table": page_table,
        "ffn1_norm": 1.0 + nrm((L, D_MODEL), 0.05),
        "ffn1_up": nrm((L, D_MODEL, 2 * D_FF), D_MODEL ** -0.5),
        "ffn1_down": nrm((L, D_FF, D_MODEL), D_FF ** -0.5),
        "mix_norm": 1.0 + nrm((L, D_MODEL), 0.05),
        "w_in": nrm((L, D_MODEL, IN_COLS), D_MODEL ** -0.5),
        "gate_bias": nrm((L, GATE_COLS), 0.01),
        "rw_mu": jax.random.uniform(next(ks), (L, RW_COLS), F32),
        "rw_w0": -0.5 + nrm((L, RW_WIDTH), 0.3),
        "rw_w2": nrm((L, DECAY_LORA, RW_WIDTH), 0.1 * DECAY_LORA ** -0.5),
        "rw_a0": nrm((L, RW_WIDTH), 0.1),
        "rw_a2": nrm((L, AAA_LORA, RW_WIDTH), 0.1 * AAA_LORA ** -0.5),
        "rw_g2": nrm((L, GATE_LORA, RW_WIDTH), GATE_LORA ** -0.5),
        "rw_k_k": 0.85 + nrm((L, RW_WIDTH), 0.05),
        "rw_k_a": 1.0 + nrm((L, RW_WIDTH), 0.05),
        "rw_r_k": nrm((L, RW_HEADS, RW_HEAD), 0.1),
        "rw_ln_w": 1.0 + nrm((L, RW_WIDTH), 0.05),
        "rw_ln_b": nrm((L, RW_WIDTH), 0.01),
        "da_lq1": nrm((L, DA_QK), 0.1),
        "da_lk1": nrm((L, DA_QK), 0.1),
        "da_lq2": nrm((L, DA_QK), 0.1),
        "da_lk2": nrm((L, DA_QK), 0.1),
        "da_subln": 1.0 + nrm((L, DA_V_WIDTH), 0.05),
        "w_proj_a": nrm((L, RW_WIDTH, D_MODEL), RW_WIDTH ** -0.5),
        "w_proj_b": nrm((L, DA_V_WIDTH, D_MODEL), DA_V_WIDTH ** -0.5),
        "w_out": nrm((L, D_MODEL, D_MODEL), D_MODEL ** -0.5),
        "ffn2_norm": 1.0 + nrm((L, D_MODEL), 0.05),
        "ffn2_up": nrm((L, D_MODEL, 2 * D_FF), D_MODEL ** -0.5),
        "ffn2_down": nrm((L, D_FF, D_MODEL), D_FF ** -0.5),
        "final_norm": 1.0 + nrm((D_MODEL,), 0.05),
    }

def reference(x_prompt, x_sample, cache_k, cache_v, state_wkv, state_shift, page_table,
              ffn1_norm, ffn1_up, ffn1_down, mix_norm, w_in, gate_bias,
              rw_mu, rw_w0, rw_w2, rw_a0, rw_a2, rw_g2, rw_k_k, rw_k_a, rw_r_k, rw_ln_w, rw_ln_b,
              da_lq1, da_lk1, da_lq2, da_lk2, da_subln, w_proj_a, w_proj_b, w_out,
              ffn2_norm, ffn2_up, ffn2_down, final_norm):
    bp, sp = x_prompt.shape[:2]
    bs, ts = x_sample.shape[:2]
    n_past = page_table.shape[1] * PAGE_SIZE
    pos_p = jnp.arange(sp, dtype=jnp.int32)
    pos_s = n_past + jnp.arange(ts, dtype=jnp.int32)
    hp, hs = x_prompt, x_sample
    kp_l, vp_l, wp_l, zp_l = [], [], [], []
    ks_l, vs_l, ws_l, zs_l = [], [], [], []
    for l in range(DEPTH):
        lp = dict(ffn1_norm=ffn1_norm[l], ffn1_up=ffn1_up[l], ffn1_down=ffn1_down[l],
                  mix_norm=mix_norm[l], w_in=w_in[l], gate_bias=gate_bias[l],
                  rw_mu=rw_mu[l], rw_w0=rw_w0[l], rw_w2=rw_w2[l], rw_a0=rw_a0[l], rw_a2=rw_a2[l],
                  rw_g2=rw_g2[l], rw_k_k=rw_k_k[l], rw_k_a=rw_k_a[l], rw_r_k=rw_r_k[l],
                  rw_ln_w=rw_ln_w[l], rw_ln_b=rw_ln_b[l], da_subln=da_subln[l],
                  w_proj_a=w_proj_a[l], w_proj_b=w_proj_b[l], w_out=w_out[l],
                  ffn2_norm=ffn2_norm[l], ffn2_up=ffn2_up[l], ffn2_down=ffn2_down[l])
        lam_init = 0.8 - 0.6 * math.exp(-0.3 * l)
        lam = (jnp.exp(jnp.sum(da_lq1[l].astype(F32) * da_lk1[l].astype(F32)))
               - jnp.exp(jnp.sum(da_lq2[l].astype(F32) * da_lk2[l].astype(F32))) + lam_init)
        ck, cv = cache_k[l], cache_v[l]
        attend_p = lambda q, k, v, lam=lam: diff_attn_prompt(q, k, v, lam)
        attend_s = lambda q, k, v, lam=lam, ck=ck, cv=cv: diff_attn_sample(q, k, v, ck, cv, page_table, lam)
        hp, kp, vp, wp, zp = decoder_layer(
            hp, pos_p, jnp.zeros((bp, RW_HEADS, RW_HEAD, RW_HEAD), hp.dtype),
            jnp.zeros((bp, RW_COLS), hp.dtype), attend_p, lp, lam_init)
        hs, k_s, v_s, w_s, z_s = decoder_layer(
            hs, pos_s, state_wkv[l], state_shift[l], attend_s, lp, lam_init)
        kp_l.append(kp); vp_l.append(vp); wp_l.append(wp); zp_l.append(zp)
        ks_l.append(k_s); vs_l.append(v_s); ws_l.append(w_s); zs_l.append(z_s)
    y_prompt = rms_norm(hp, final_norm)
    y_sample = rms_norm(hs, final_norm)
    k_prompt, v_prompt = jnp.stack(kp_l), jnp.stack(vp_l)
    wkv_prompt, shift_prompt = jnp.stack(wp_l), jnp.stack(zp_l)
    k_sample, v_sample = jnp.stack(ks_l), jnp.stack(vs_l)
    wkv_sample, shift_sample = jnp.stack(ws_l), jnp.stack(zs_l)
    return (y_prompt, y_sample, k_prompt, v_prompt, wkv_prompt, shift_prompt,
            k_sample, v_sample, wkv_sample, shift_sample)


_drawn_inputs = setup_inputs


def setup_inputs(seed=0):
    import zlib

    import numpy as np

    out = dict(_drawn_inputs(seed))
    spreads = {}
    factors = {'gate_bias': 8.0,
     'rw_w2': 4.6,
     'rw_k_k': 36.398,
     'rw_ln_w': 4.221,
     'rw_ln_b': 29.877,
     'da_lq1': 8.0,
     'da_lk1': 8.0,
     'da_subln': 2.884,
     'ffn2_norm': 3.083}
    for name, (base, spread) in spreads.items():
        noise = np.random.default_rng([zlib.crc32(name.encode()), seed]).standard_normal(out[name].shape)
        drawn = base * np.exp(spread * noise) if base else spread * noise
        out[name] = __import__('jax').numpy.asarray(drawn.astype(out[name].dtype))
    for name, factor in factors.items():
        out[name] = (out[name] * factor).astype(out[name].dtype)
    return out
```

```python
import concourse.bass as bass
from concourse import mybir
from concourse.alu_op_type import AluOpType as ALU
from contextlib import ExitStack
import math
import numpy as np

F32 = mybir.dt.float32
F32R = mybir.dt.float32r
I32 = mybir.dt.int32
ACT = mybir.ActivationFunctionType
AX = mybir.AxisListType.X
ds = bass.ds

P = 128
D = 1024
KT = D // P
NP = 1024
NS = 8
NT = NP + NS
NCH = 3
CH = NT // NCH
FT = 22
GROUP = 8
RW = 512
RW_COLS = 3 * RW + 256
ZT = RW_COLS // P
HP = 4
QT0, VT0, GT0 = ZT, ZT + 2 * HP, ZT + 3 * HP
GT = 2 * KT
C = 64
NC = NP // C
PAGES = 16
PAGE = 128
N_PHYS = 160
EPS = 1e-6
GN_EPS = 1e-5 * 64 * 64
LAM_INIT = 0.8 - 0.6 * math.exp(0.0)
SCALE = 64 ** -0.5
LOGDECAY = -math.exp(-0.5)
LEVELS = 5

PARAMS = [("ffn1_norm", 8), ("mix_norm", 8), ("ffn2_norm", 8), ("final_norm", 8), ("gate_bias", 16),
          ("rw_mu", ZT), ("rw_w0", 4), ("rw_a0", 4), ("rw_k_k", 4), ("rw_k_a", 4), ("rw_r_k", 4),
          ("rw_ln_w", 4), ("rw_ln_b", 4), ("da_subln", 4)]
ROW = {}
NROWS = 0
for _name, _n in PARAMS:
    ROW[_name] = NROWS
    NROWS += _n
ROW["lambda"] = NROWS
NROWS += 2

CONST_COLS = [("ident", 128), ("ones", 128), ("block_ones", 128), ("top_ones", 128), ("bottom_ones", 128),
              ("causal", 128), ("ident_stack", 64), ("strict_st", 64), ("incl_st", 64),
              ("pair_ts", 64), ("pair_st", 64)] + [(f"level{l}", 64) for l in range(LEVELS)]
CONST_AT = {}
NCONST = 0
for _name, _n in CONST_COLS:
    CONST_AT[_name] = NCONST
    NCONST += _n


def shape_constants():
    table = np.zeros((P, NCONST), np.float32)
    r = np.arange(P)

    def put(name, a):
        table[:, CONST_AT[name]:CONST_AT[name] + a.shape[1]] = a
    put("ident", np.eye(P))
    put("ones", np.ones((P, P)))
    put("block_ones", (r[:, None] // 64 == r[None, :] // 64) * 1.0)
    put("top_ones", (r[:, None] < 64) * np.ones((P, P)))
    put("bottom_ones", (r[:, None] >= 64) * np.ones((P, P)))
    put("causal", np.where(r[None, :] <= r[:, None], 0.0, -1e30))
    s, t = r[:, None] % 64, np.arange(64)[None, :]
    put("ident_stack", (s == t) * 1.0)
    put("strict_st", (s < t) * 1.0)
    put("incl_st", (s <= t) * 1.0)
    put("pair_ts", ((s // 2 == t // 2) & (s > t)) * 1.0)
    put("pair_st", ((s // 2 == t // 2) & (s < t)) * 1.0)
    for l in range(LEVELS):
        half = 2 << l
        put(f"level{l}", ((s // (2 * half) == t // (2 * half)) & (s // half % 2 == 0) & (t // half % 2 == 1)) * 1.0)
    pos = np.concatenate([np.arange(NP), np.full(NS, PAGES * PAGE)]).astype(np.float32)
    inv = (np.float32(10000.0) ** (-np.arange(32, dtype=np.float32) / np.float32(32))).astype(np.float32)
    ang = (pos[None, :] * inv[r % 32][:, None]).astype(np.float32)
    sign = np.where(r % 64 < 32, 1.0, -1.0).astype(np.float32)[:, None]
    rot = np.stack([np.cos(ang), np.sin(ang) * sign], 1).astype(np.float32)
    fresh = np.broadcast_to((np.arange(NP) % C != 0).astype(np.float32), (P, NP)).copy()
    return table, rot, fresh


LINES = [
    [("x_saved", 16), ("gate_saved0", 8 * GT)],
    [("rotary_loaded", 16), ("gate_saved1", 8 * GT)],
    [("x_moved1", 4), ("lam_exp", 1), ("k_tok_made", 9), ("probs_made", 64), ("q_bc", NS), ("s_exp", 2), ("o_sq", HP),
     ("z_act", 2), ("lora_act", 2 * HP), ("ck_p", 2 * NC), ("y_sq", HP), ("yb_high", HP), ("merge_high", KT), ("y_moved1", 4)],
    [("w_lo_moved", 32), ("o_root", HP), ("kk_sq", HP), ("ck_tok_moved", 4 * NC), ("y_root", HP)],
    [("o_moved", 32), ("w_sample", HP), ("ck_r_moved", NC), ("ya_high", HP)],
    [("kk_norm", HP), ("ck_t1_act", LEVELS * NC)],
    [("par_trans", 1), ("x_trans", KT), ("lam_sums", 1), ("v_trans", 9), ("scores_done", 32), ("s_self", 1),
     ("q_rows", NS), ("s_sum", 1), ("o_sq_sum", HP), ("z_rows_trans", 1), ("lora_made", HP), ("ck_gram", NC),
     ("wkv_trans", 1), ("rows_made", HP), ("y_sum", HP), ("y_trans", 9)],
    [("k_trans", 9), ("w_trans_lo", 32), ("kk_sum", HP), ("ck_tok", NC), ("y_sq_sum", HP)],
    [("w_trans_hi", 16), ("ck_r", NC), ("bonus_sum", HP)],
    [("o_done", 32), ("ck_t1", LEVELS * NC), ("g_made", HP)],
    [("par_moved", 2), ("x_moved0", 4), ("v_tok_made", 9), ("neg_max", 32), ("s_self_prod", 1),
     ("s_self_moved", 2), ("q_diag", NS), ("s_max_part", 1), ("s_shifted", 2), ("s_sum_part", 1),
     ("s_weights", 2), ("o_sample", NS), ("o_mean", HP), ("z_last", ZT), ("z_rows_made", 1),
     ("kk_scaled", HP), ("ck_zeroed", 1), ("ck_at", NC), ("wkv_made", 2), ("row_diag", 5 * HP),
     ("y_centred", HP), ("yb_split", HP), ("merge_full", KT), ("y_moved0", 5)],
    [("lam_prod", 1), ("yb_done", HP),
     ("ld_made", HP), ("ck_bt", NC), ("state_new", HP), ("y_var", HP)],
    [("ck_kt", NC),
     ("bonus_prod", HP), ("merged", KT)],
    [("ck_rt", NC)],
    [("pre_done", HP), ("y_final", HP)],
    [("ck_x", NC), ("ya_split", HP)],
    [("w_ready", 32), ("ck_aak", 2 * NC)],
    [("w_hi_moved", 16), ("ck_ar", 2 * NC)],
]


PRIMED = {
    "scalar": ["ck_y_out"],
    "vector": ["w_split0", "w_split1", "psum_free0", "psum_free1", "ff_full", "z_mixed0", "z_mixed1",
               "k_used0", "k_used1", "k_used2", "k_used3", "ck_state"],
    "tensor": ["unit_done0", "unit_done1", "v_used0", "v_used1", "v_used2", "v_used3"],
}


class Events(dict):
    def __init__(self, nc, ctx):
        super().__init__()
        self.nc, self.ctx, self.base = nc, ctx, {}
        for line in LINES:
            shared, total = self.make(line[0][0]), 0
            for name, n in line:
                self[name], self.base[name] = shared, total
                total += n
        for names in PRIMED.values():
            self.base.update((name, 1) for name in names)

    def prime(self, eng, engine):
        for name in PRIMED[engine]:
            eng.sem_inc(self[name], 1)

    def make(self, name):
        return self.ctx.enter_context(self.nc.semaphore("s_" + name))

    def __missing__(self, name):
        self[name] = self.make(name)
        return self[name]

    def at(self, name, n):
        return self[name], n + self.base.get(name, 0)


def build(nc, A):
    ctx = ExitStack()
    with ctx:
        ev = Events(nc, ctx)

        base = (nc.sbuf_base + 63) // 64 * 64
        TILE = NT * 4
        place = [base]

        def at(name, cols, offset=None, dt=F32):
            if offset is None:
                offset = place[0]
                place[0] = (place[0] + cols * 4 + 31) // 32 * 32
            return nc.alloc_sbuf_tensor_at(name, [P, cols], dt, offset=offset)

        stg = [at(f"w_stage{s}", KT * P)[:, :].rearrange("p (k n) -> p k n", n=P) for s in range(2)]
        whi = [at(f"w_hi{s}", KT * P, dt=F32R)[:, :].rearrange("p (k n) -> p k n", n=P) for s in range(2)]
        wlo = [at(f"w_lo{s}", KT * P, dt=F32R)[:, :].rearrange("p (k n) -> p k n", n=P) for s in range(2)]
        arena = place[0]
        place[0] += 40 * TILE

        def tiles(name, first, n, dt=F32):
            return at(name, n * NT, arena + first * TILE, dt)[:, :].rearrange("p (k n) -> p k n", n=NT)

        def cols(name, first, n):
            return at(name, n, arena + first * TILE)[:, :]

        T = at("tmp", 2 * NT)[:, :].rearrange("p (s n) -> p s n", n=NT)
        rstd = at("rstd", NT)[:, :]
        const = at("const", NCONST)[:, :]
        par = at("par", NROWS)[:, :]
        zlast = at("z_last", 9 * ZT)[:, :].rearrange("p (j m) -> p j m", m=ZT)
        zshift = at("z_shift", NS * ZT)[:, :].rearrange("p (b m) -> p b m", m=ZT)
        vsam = at("v_sample", HP * NS)[:, :].rearrange("p (h b) -> p h b", b=NS)
        small = at("small", 64)[:, :]
        idle = at("idle", 4)[:, :]
        wsam = at("decay_sample", HP * NS)[:, :].rearrange("p (h b) -> p h b", b=NS)
        ptab = nc.alloc_sbuf_tensor_at("pages", [1, NS * PAGES], I32, offset=place[0])
        place[0] += NS * PAGES * 4
        assert place[0] <= nc.sbuf_usable_end, (place[0], nc.sbuf_usable_end)

        def K(name, n=None):
            width = n or dict(CONST_COLS)[name]
            return const[:, CONST_AT[name]:CONST_AT[name] + width]

        def param(name, i=0, n=1):
            return par[:, ROW[name] + i:ROW[name] + i + n]

        X = tiles("x_res", 0, KT)
        H = [tiles("h_hi", 8, KT, F32R), tiles("h_lo", 16, KT, F32R)]
        G = [tiles("ff_hi", 24, GROUP, F32R), tiles("ff_lo", 32, GROUP, F32R)]
        xin = cols("x_in", 24, 9 * D).rearrange("p (t n) -> p t n", n=D)
        prow = cols("param_rows", 38, P)
        srow = cols("shift_rows", 39, P)
        Q = tiles("q_rot", 0, HP)
        Kr = tiles("k_rot", 4, HP)
        Vt = tiles("v_feat", 24, HP)
        rot = tiles("rotary", 28, 2)
        Vtok = cols("v_tok", 30, 8 * 512).rearrange("p (t n) -> p t n", n=512)
        pr = tiles("probs", 34, 4)[:, :, 0:NP].rearrange("p (s m) n -> p s m n", m=2)
        wT = [cols(f"w_trans{s}", 38 + s, NP) for s in range(2)]
        kout = [cols(f"k_out{s}", 34 + s, 512) for s in range(2)]
        ring = cols("kv_ring", 30, 16 * 512).rearrange("p (g j n) -> p g j n", g=4, j=4)
        prod = cols("kq_prod", 24, 4 * 512)
        SC = cols("score_sums", 26, 1024)
        Wp = cols("s_weights", 27, 512)
        Qbc = tiles("q_bcast", 27, 1)[:, 0, 512:1024]
        Qdg = cols("q_diag", 28, 512)
        sm = cols("s_small", 29, 512)
        smax, sself, ssum, sexp = sm[:, 0:64], sm[:, 64:128], sm[:, 128:192], sm[:, 192:256]
        wself, qk_cols = sm[:, 256:288], sm[:, 320:352]
        smaxp, vw = sm[:, 352:416], sm[:, 416:420]
        Z = tiles("z_mix", 24, ZT)
        Rf, Kf, Vf = Z[:, 0:4], Z[:, 4:8], Z[:, 8:12]
        CUM = tiles("cum_y", 4, HP)
        KKn = tiles("kk", 16, HP)
        Bf = tiles("b_vec", 20, HP)
        lw2 = cols("lora_w2a2", 38, 512)
        lg2 = cols("lora_g2", 39, 512)
        fresh = cols("fresh", 15, NP)
        wk = at("chunk_work", 8 * NT, arena + 8 * TILE)[:, :]
        wk2 = at("chunk_work2", 2 * NT, arena + 38 * TILE)[:, :]
        used = [0, 0]

        def work(n, two=False):
            w, i = (wk2, 1) if two else (wk, 0)
            assert used[i] + n <= (2 if two else 8) * NT
            used[i] += n
            return w[:, used[i] - n:used[i]]

        def h4(a):
            return a.rearrange("p (h n) -> p h n", h=HP)
        Pb = h4(work(HP * 65))
        Pinv = h4(work(256))
        ar = work(512).rearrange("p (h a t) -> p h a t", h=HP, a=2)
        bts, kts = h4(work(256)), h4(work(256))
        bd_first = used[0]
        atd, btd, ktd, vtd = [h4(work(512)) for _ in range(4)]
        aakd, btmd = h4(work(512)), [h4(work(512)) for _ in range(2)]
        Yd, T1d, Ud, Sd = [h4(work(512)) for _ in range(4)]
        bd_last = used[0]
        btok, ktok = h4(work(512)), h4(work(512))
        vts, Ys = h4(T[:, 1, 0:256]), h4(T[:, 1, 256:512])
        vtok = h4(work(512, True))
        LTs, arbs, arks, Xs, T1s = [h4(work(256, True)) for _ in range(5)]
        Rs, Us, Ss = h4(T[:, 0, 0:256]), h4(T[:, 0, 256:512]), h4(T[:, 0, 512:768])
        St = cols("state", 8, HP * 512).rearrange("p (h b j) -> p h b j", h=HP, b=NS)
        dg = cols("row_diag", 10, 5 * 512).rearrange("p (v b j) -> p v b j", v=5, b=NS)
        stm = cols("state_tmp", 13, 512).rearrange("p (b j) -> p b j", b=NS)
        sa = small[:, 8:16]
        wfin = cols("wkv_out", 14, HP * 64).rearrange("p (h n) -> p h n", h=HP)
        zrow = cols("z_rows", 14, P)
        G2 = cols("lora_g2b", 15, 512)
        YA = [tiles("ya_hi", 16, HP, F32R), tiles("ya_lo", 20, HP, F32R)]
        YB = [tiles("yb_hi", 8, HP, F32R), tiles("yb_lo", 12, HP, F32R)]
        M = [tiles("merged_hi", 32, KT, F32R), tiles("merged_lo", 24, KT, F32R)]
        gring = tiles("gate_ring", 4, 4).rearrange("p (s a) n -> p s a n", a=2)
        yout = [cols(f"y_out{s}", 24 + s, D) for s in range(2)]

        x_save = nc.dram_tensor("x_save", (KT, P, NT), F32).ap()
        g_save = nc.dram_tensor("gate_save", (GT, P, NT), F32).ap()

        PS = ctx.enter_context(nc.psum_tensor("ps", [P, 8, 512], F32))
        PSf = PS[:, :, :].rearrange("p a n -> p (a n)")
        dense = [PS[:, 3 * s:3 * s + 3, 0:CH] for s in range(2)]

        def ch3(a):
            return a.rearrange("p (c n) -> p c n", c=NCH)

        def ps4(bank, first=0, n=64):
            return PS[:, bank, first:first + HP * n].rearrange("p (h n) -> p h n", h=HP)

        def rows(name):
            return A[name].rearrange("(r n) -> r n", n=P) if len(A[name].shape) == 1 else \
                A[name].rearrange("l (r n) -> (l r) n", n=P)

        w_in = A["w_in"][0]
        wsrc = {n: A[n][0].rearrange("(k p) n -> p k n", p=P)
                for n in ("ffn1_up", "ffn1_down", "ffn2_up", "ffn2_down", "w_in", "w_proj_a", "w_proj_b", "w_out")}
        ck = A["cache_k"].rearrange("l n t m d -> (l n) t (m d)")
        cv = A["cache_v"].rearrange("l n t h d -> (l n) t (h d)")

        GROUPS = [(0, 8), (8, 8), (16, 6)]
        PAIRS_FFN = FT + len(GROUPS) * KT // 2
        AT_QK = PAIRS_FFN
        AT_V = AT_QK + HP
        AT_GATES = AT_V + HP // 2
        AT_Z = AT_GATES + GT // 2
        AT_MERGE = AT_Z + ZT // 2
        AT_OUT = AT_MERGE + KT // 2
        AT_FFN2 = AT_OUT + KT // 2

        def loop(eng, n, body, end=False):
            if n - end > 0:
                with eng.Fori(0, n - end) as i:
                    body(i, False)
            if end:
                body(n - 1, True)

        def flat(a):
            return a.rearrange("p a n -> p (a n)")

        def bc(a, n):
            return a.broadcast_to([a.shape[0], a.shape[1], n])

        def over_heads(a):
            return a.unsqueeze(1).broadcast_to([a.shape[0], HP, a.shape[1]])

        halves = (slice(0, 64), slice(64, 128))

        def settle(eng):
            if eng is nc.scalar:
                nc.scalar.activation(idle[:, 0:1], idle[:, 1:2], ACT.Copy)
            else:
                nc.gpsimd.tensor_tensor(idle[:, 2:3], idle[:, 1:2], idle[:, 1:2], ALU.add)
            eng.drain()

        VIEW_SC = SC.rearrange("p (b g m) -> p b g m", b=NS, g=PAGES)
        VIEW_W = Wp.rearrange("p (b g h) -> p b g h", b=NS, g=PAGES)

        block = ctx.enter_context(nc.Block())

        @block.sync
        def _(sp):
            def load_unit(s, c, src, nk=KT, second=None):
                sp.wait_ge(*ev.at(f"w_split{s}", c))
                h = HP
                sp.dma_start(stg[s][:, 0:h, :], src[:, 0:h]).then_inc(ev[f"w_loaded{s}"], 16)
                sp.dma_start(stg[s][:, h:nk, :], src[:, h:nk] if second is None else second)\
                    .then_inc(ev[f"w_loaded{s}"], 16)

            sp.dma_start(const, A["const_table"]).then_inc(ev["params_loaded"], 16)
            for name, n in PARAMS:
                src = A[name].rearrange("l h n -> l (h n)") if name == "rw_r_k" else A[name]
                src = src.rearrange("(r n) -> r n", n=P) if len(src.shape) == 1 else \
                    src.rearrange("l (r n) -> (l r) n", n=P)
                sp.dma_start(prow[ROW[name]:ROW[name] + n, :], src).then_inc(ev["params_loaded"], 16)
            for i, name in enumerate(("da_lq1", "da_lq2", "da_lk1", "da_lk2")):
                r = ROW["lambda"] + i // 2
                sp.dma_start(prow[r:r + 1, (i % 2) * 64:(i % 2) * 64 + 64], A[name])\
                    .then_inc(ev["params_loaded"], 16)
            sp.dma_start(srow[0:NS * ZT, :], A["state_shift"][0].rearrange("b (m p) -> (b m) p", p=P))\
                .then_inc(ev["params_loaded"], 16)
            sp.dma_start(ptab[:, :], A["page_table"].rearrange("(a b) n -> a (b n)", a=1))\
                .then_inc(ev["pages_loaded"], 16)
            for t in range(8):
                sp.dma_start(xin[:, t, :], A["x_prompt"][0, t * P:(t + 1) * P, :]).then_inc(ev["x_loaded"], 16)
            sp.dma_start(xin[0:NS, 8, :], A["x_sample"][:, 0, :]).then_inc(ev["x_loaded"], 16)

            def ffn_loads(first, up, down):
                for j0, n in GROUPS:
                    with sp.Fori(0, n) as i:
                        for s in range(2):
                            load_unit(s, i + first, wsrc[up][:, :, ds((i + (j0 + s * FT)) * P, P)])
                    first += n
                    with sp.Fori(0, KT // 2) as i:
                        for s in range(2):
                            load_unit(s, i + first, wsrc[down][:, j0:j0 + n, ds((i * 2 + s) * P, P)], n)
                    first += KT // 2

            def w_loads(first, name, tile, n):
                with sp.Fori(0, n // 2) as i:
                    for s in range(2):
                        load_unit(s, i + first, wsrc[name][:, :, ds((i * 2 + (tile + s)) * P, P)])

            ffn_loads(0, "ffn1_up", "ffn1_down")
            w_loads(AT_QK, "w_in", QT0, 3 * HP)
            w_loads(AT_GATES, "w_in", GT0, GT)

            sp.wait_ge(*ev.at("pages_loaded", 16))
            sp.wait_ge(*ev.at("o_done", 8 * HP))
            sp.wait_ge(*ev.at("v_stored", 16 * 9))
            sp.wait_ge(*ev.at("k_stored0", 16 * 5))
            sp.wait_ge(*ev.at("k_stored1", 16 * 4))
            for what, cache in enumerate((ck, cv)):
                with sp.Fori(0, NS) as b:
                    for g in range(4):
                        if what == 0:
                            sp.wait_ge(*ev.at(f"k_used{g}", b))
                        else:
                            sp.wait_ge(*ev.at(f"k_used{g}", NS))
                            sp.wait_ge(*ev.at(f"v_used{g}", b))
                        for j in range(4):
                            page = sp.value_load(ptab[0:1, ds(b * PAGES + (4 * g + j), 1)],
                                                 min_val=0, max_val=N_PHYS - 1)
                            sp.dma_start(ring[:, g, j, :], cache[ds(page, 1)].rearrange("a t n -> (a t) n"))\
                                .then_inc(ev[f"page_loaded{g}"], 16)
            w_loads(AT_Z, "w_in", 0, ZT)
            sp.wait_ge(*ev.at("unit_done1", AT_MERGE))
            sp.wait_ge(*ev.at("v_used3", NS))
            sp.dma_start(lw2[0:64, :], A["rw_w2"][0]).then_inc(ev["lora_loaded"], 16)
            sp.dma_start(lw2[64:128, :], A["rw_a2"][0]).then_inc(ev["lora_loaded"], 16)
            sp.dma_start(fresh, A["const_fresh"]).then_inc(ev["lora_loaded"], 16)
            sp.wait_ge(*ev.at("wkv_trans", 1))
            for h in range(HP):
                for b in range(NS):
                    sp.dma_start(St[:, h, b, :],
                                 A["state_wkv"][0, b].rearrange("h i j -> (h i) j")[h * P:(h + 1) * P, :])\
                        .then_inc(ev["state_loaded"], 16)
            sp.dma_start(G2, A["rw_g2"][0]).then_inc(ev["g2_loaded"], 16)
            with sp.Fori(0, KT // 2) as i:
                for s in range(2):
                    load_unit(s, i + AT_MERGE, wsrc["w_proj_a"][:, :, ds((i * 2 + s) * P, P)],
                              second=wsrc["w_proj_b"][:, :, ds((i * 2 + s) * P, P)])
            w_loads(AT_OUT, "w_out", 0, KT)
            ffn_loads(AT_FFN2, "ffn2_up", "ffn2_down")

        @block.gpsimd
        def _(pool):
            pool.wait_ge(*ev.at("h_ready", 2 * KT))
            pool.dma_start(x_save.rearrange("k p n -> p k n"), X).then_inc(ev["x_saved"], 16)
            pool.dma_start(rot, A["const_rotary"]).then_inc(ev["rotary_loaded"], 16)
            with pool.Fori(0, GT // 2) as i:
                for s in range(2):
                    pool.wait_ge(*ev.at(f"psum_free{s}", i + (AT_GATES + 1)))
                    pool.dma_start(g_save[ds(i * 2 + s, 1)].rearrange("a p n -> (a p) n"), T[:, s, :])\
                        .then_inc(ev[f"gate_saved{s}"], 16)
            for t in range(9):
                n = P if t < 8 else NS
                pool.wait_ge(*ev.at("v_tok_made", t + 1))
                src = Vtok[:, t, :] if t < 8 else wT[1][:, 0:512]
                dst = A["v_prompt"][0, 0, t * P:(t + 1) * P].rearrange("t h d -> t (h d)") if t < 8 else \
                    A["v_sample"][0, :, 0].rearrange("t h d -> t (h d)")
                pool.dma_start(dst, src[0:n, :]).then_inc(ev["v_stored"], 16)
                pool.wait_ge(*ev.at("k_tok_made", t + 1))
                dst = A["k_prompt"][0, 0, t * P:(t + 1) * P].rearrange("t m d -> t (m d)") if t < 8 else \
                    A["k_sample"][0, :, 0].rearrange("t m d -> t (m d)")
                pool.dma_start(dst, kout[t % 2][0:n, :]).then_inc(ev[f"k_stored{t % 2}"], 16)
            pool.wait_ge(*ev.at("s_max_part", 1))
            nc.gpsimd.partition_all_reduce(smax, smaxp, P, bass.bass_isa.ReduceOp.max).then_inc(ev["s_max_all"], 1)
            pool.wait_ge(*ev.at("z_rows_made", 1))
            pool.dma_start(A["shift_prompt"][0].rearrange("b (m p) -> (b m) p", p=P), zrow[0:ZT, :])\
                .then_inc(ev["z_stored"], 16)
            pool.dma_start(A["shift_sample"][0].rearrange("b (m p) -> (b m) p", p=P), zrow[ZT:9 * ZT, :])\
                .then_inc(ev["z_stored"], 16)
            pool.wait_ge(*ev.at("ck_zeroed", 1))
            with pool.Fori(0, NC) as c:
                for dst, src, ready in ((atd, ar[:, :, 0, :], "ck_at"), (btd, bts, "ck_bt"), (ktd, kts, "ck_kt")):
                    pool.wait_ge(*ev.at(ready, c + 1))
                    settle(nc.gpsimd)
                    for q in halves:
                        nc.gpsimd.tensor_copy(dst[q, :, q], src[q])
                        pool.drain()
                for q in halves:
                    nc.gpsimd.tensor_copy(vtd[q, :, q], Vf[q, :, ds(c * C, C)]).then_inc(ev["ck_diag"], 1)
                    pool.drain()
            pool.wait_ge(*ev.at("wkv_made", 2))
            for two in range(2):
                pool.dma_start(A["wkv_prompt"][0, 0].rearrange("(h two) i j -> two i h j", two=2)[two],
                               wfin[halves[two]]).then_inc(ev["wkv_stored"], 16)
            for h in range(HP):
                pool.wait_ge(*ev.at("state_new", h + 1))
                for b in range(NS):
                    pool.dma_start(A["wkv_sample"][0, b].rearrange("h i j -> (h i) j")[h * P:(h + 1) * P, :],
                                   St[:, h, b, :]).then_inc(ev["state_stored"], 16)
            pool.wait_ge(*ev.at("ya_split", HP))
            pool.wait_ge(*ev.at("gate_saved0", 16 * (GT // 2)))
            pool.wait_ge(*ev.at("gate_saved1", 16 * (GT // 2)))
            with pool.Fori(0, KT // 2) as i:
                for s in range(2):
                    pool.wait_ge(*ev.at(f"psum_free{s}", i + AT_MERGE))
                    for a in range(2):
                        pool.dma_start(gring[:, s, a, :],
                                       g_save[ds(i * 2 + (s + a * KT), 1)].rearrange("a p n -> (a p) n"))\
                            .then_inc(ev[f"gates_back{s}"], 16)
            pool.wait_ge(*ev.at("merged", KT))
            pool.wait_ge(*ev.at("x_saved", 16))
            pool.dma_start(X, x_save.rearrange("k p n -> p k n")).then_inc(ev["x_back"], 16)
            for t in range(9):
                pool.wait_ge(*ev.at(f"y_moved{t % 2}", t // 2 + 1))
                dst = A["y_prompt"][0, t * P:(t + 1) * P, :] if t < 8 else A["y_sample"][:, 0, :]
                pool.dma_start(dst, yout[t % 2][0:P if t < 8 else NS, :]).then_inc(ev[f"y_stored{t % 2}"], 16)
            for name, n in (("y_stored0", 5), ("y_stored1", 4), ("v_stored", 9), ("k_stored0", 5), ("k_stored1", 4),
                            ("z_stored", 2), ("wkv_stored", 2), ("state_stored", HP * NS)):
                pool.wait_ge(*ev.at(name, 16 * n))

        @block.scalar
        def _(act):
            ev.prime(act, "scalar")
            sc = nc.scalar

            def split(s, c):
                act.wait_ge(*ev.at(f"w_loaded{s}", (c + 1) * 32))
                act.wait_ge(*ev.at(f"unit_done{s}", c))
                sc.activation(whi[s], stg[s], ACT.Copy).then_inc(ev[f"w_high{s}"], 1)

            for k in range(1, KT, 2):
                act.wait_ge(*ev.at("x_trans", k + 1))
                sc.activation(X[:, k, :], PSf[:, 1536:1536 + NT], ACT.Copy).then_inc(ev["x_moved1"], 1)

            def norm(n, high=True):
                for k in range(KT):
                    if k == 0:
                        act.wait_ge(*ev.at("x_done", n + 1))
                    if k >= 2:
                        act.wait_ge(*ev.at("sq_used", n * KT + k - 1))
                    sc.activation(T[:, k % 2, :], X[:, k, :], ACT.Square).then_inc(ev["sq_made"], 1)
                act.wait_ge(*ev.at("mean_made", n + 1))
                sc.activation(rstd, rstd, ACT.Sqrt).then_inc(ev["root_made"], 1)
                if high:
                    for k in range(KT):
                        act.wait_ge(*ev.at("h_full", n * KT + k + 1))
                        sc.activation(H[0][:, k, :], T[:, k % 2, :], ACT.Copy).then_inc(ev["h_high"], 1)

            def ffn(first, pairs, last):
                for gi, (j0, n) in enumerate(GROUPS):
                    def up(i, end):
                        c = i + first
                        split(1, c)
                        act.wait_ge(*ev.at("unit_done0", c + 1))
                        act.wait_ge(*ev.at("ff_full", i + pairs))
                        sc.activation(ch3(T[:, 0, :]), dense[0], ACT.Silu).then_inc(ev["psum_free0"], 1)
                        split(0, c + 1)
                        act.wait_ge(*ev.at("ff_full", i + (pairs + 1)))
                        settle(nc.scalar)
                        sc.activation(flat(G[0][:, ds(i, 1), :]), T[:, 1, :], ACT.Copy).then_inc(ev["ff_high"], 1)
                    loop(act, n, up)
                    first += n
                    pairs += n

                    def down(i, end):
                        split(1, i + first)
                        if not end:
                            split(0, i + (first + 1))
                    loop(act, KT // 2, down, last and gi == len(GROUPS) - 1)
                    first += KT // 2

            norm(0)
            split(0, 0)
            ffn(0, 0, False)
            norm(1)

            def qk(i, end):
                split(1, i + AT_QK)
                split(0, i + (AT_QK + 1))
            loop(act, HP, qk)

            def values(i, end):
                for s in range(2):
                    split(1 - s, i + (AT_V + s))
                    act.wait_ge(*ev.at(f"unit_done{s}", i + (AT_V + 1)))
                    settle(nc.scalar)
                    sc.activation(flat(Vt[:, ds(i * 2 + s, 1), :]).rearrange("p (c n) -> p c n", c=NCH), dense[s],
                                  ACT.Copy).then_inc(ev[f"psum_free{s}"], 1)
            loop(act, HP // 2, values)

            def gates(i, end):
                for s in range(2):
                    if s == 0 or not end:
                        split(1 - s, i + (AT_GATES + s))
                    act.wait_ge(*ev.at(f"unit_done{s}", i + (AT_GATES + 1)))
                    act.wait_ge(*ev.at(f"gate_saved{s}", 16 * i))
                    settle(nc.scalar)
                    sc.activation(ch3(T[:, s, :]), dense[s], ACT.Sigmoid,
                                  bias=par[:, ds(i * 2 + (ROW["gate_bias"] + s), 1)]).then_inc(ev[f"psum_free{s}"], 1)
            act.wait_ge(*ev.at("rope_done", 2 * HP))
            loop(act, GT // 2, gates, True)

            act.wait_ge(*ev.at("lam_sums", 1))
            sc.activation(small[:, 0:2], PS[:, 7, 0:2], ACT.Exp).then_inc(ev["lam_exp"], 1)
            for t in range(9):
                n = P if t < 8 else NS
                act.wait_ge(*ev.at("k_trans", t + 1))
                if t >= 2:
                    act.wait_ge(*ev.at(f"k_stored{t % 2}", 16 * (t // 2)))
                sc.activation(kout[t % 2][0:n, :], PS[0:n, 2 + t % 2, :], ACT.Copy).then_inc(ev["k_tok_made"], 1)
            act.wait_ge(*ev.at("k_stored0", 16 * 5))
            act.wait_ge(*ev.at("k_stored1", 16 * 4))
            act.wait_ge(*ev.at("v_stored", 16 * 9))

            for step in range(8 * HP):
                qi, s = step // HP, step % 2
                n = (qi + 1) * P
                act.wait_ge(*ev.at("neg_max", step + 1))
                if step >= 2:
                    act.wait_ge(*ev.at("o_done", step - 1))
                for m in range(2):
                    sc.activation(pr[:, s, m, 0:n], PSf[:, m * 1024:m * 1024 + n], ACT.Exp,
                                  bias=small[:, 16 + 4 * s + m:17 + 4 * s + m], scale=SCALE,
                                  accum_out=small[:, 18 + 4 * s + m:19 + 4 * s + m]).then_inc(ev["probs_made"], 1)
                act.wait_ge(*ev.at("w_trans_lo", step + 1))
                lo = min(4, qi + 1) * P
                sc.activation(wT[s][:, 0:lo], PS[:, 4, 0:lo], ACT.Copy).then_inc(ev["w_lo_moved"], 1)
                act.wait_ge(*ev.at("o_done", step + 1))
                sc.activation(Q[:, step % HP, qi * P:(qi + 1) * P], PS[:, 6 + s, 0:P], ACT.Copy)\
                    .then_inc(ev["o_moved"], 1)

            with act.Fori(0, NS) as b:
                act.wait_ge(*ev.at("q_rows", b + 1))
                act.wait_ge(*ev.at("k_used3", b))
                sc.activation(Qbc, PS[:, 6, :], ACT.Copy).then_inc(ev["q_bc"], 1)
            act.wait_ge(*ev.at("s_shifted", 2))
            sc.activation(SC, SC, ACT.Exp, scale=SCALE).then_inc(ev["s_exp"], 1)
            sc.activation(sexp, sself, ACT.Exp, scale=SCALE).then_inc(ev["s_exp"], 1)
            for h in range(HP):
                act.wait_ge(*ev.at("o_sample", NS))
                if h >= 2:
                    act.wait_ge(*ev.at("o_mean", h - 1))
                sc.activation(T[:, h % 2, :], Q[:, h, :], ACT.Square).then_inc(ev["o_sq"], 1)
                act.wait_ge(*ev.at("o_mean", h + 1))
                sc.activation(rstd, rstd, ACT.Sqrt).then_inc(ev["o_root"], 1)

            act.wait_ge(*ev.at("yb_done", HP))
            split(0, AT_Z)

            def z_raw(i, end):
                for s in range(2):
                    if s == 0 or not end:
                        split(1 - s, i + (AT_Z + s))
                    act.wait_ge(*ev.at(f"unit_done{s}", i + (AT_Z + 1)))
                    act.wait_ge(*ev.at(f"z_mixed{s}", i))
                    sc.activation(ch3(T[:, s, :]), dense[s], ACT.Copy).then_inc(ev[f"psum_free{s}"], 1)
            loop(act, ZT // 2, z_raw, True)

            act.wait_ge(*ev.at("z_mixed0", ZT // 2))
            act.wait_ge(*ev.at("z_mixed1", ZT // 2))
            sc.activation(Z[0:64, 12, :], Z[0:64, 12, :], ACT.Tanh).then_inc(ev["z_act"], 1)
            sc.activation(Z[:, 13, :], Z[:, 13, :], ACT.Sigmoid).then_inc(ev["z_act"], 1)
            for h in range(HP):
                act.wait_ge(*ev.at("lora_made", h + 1))
                act.wait_ge(*ev.at("pre_done", h))
                sc.activation(ch3(T[:, 0, :]), dense[0], ACT.Sigmoid, bias=param("rw_w0", h)).then_inc(ev["lora_act"], 1)
                sc.activation(ch3(Bf[:, h, :]), dense[1], ACT.Sigmoid, bias=param("rw_a0", h)).then_inc(ev["lora_act"], 1)
                act.wait_ge(*ev.at("kk_scaled", h + 1))
                sc.activation(T[:, 1, :], KKn[:, h, :], ACT.Square).then_inc(ev["kk_sq"], 1)
                act.wait_ge(*ev.at("ld_made", h + 1))
                sc.activation(wsam[:, h, :], T[:, 0, NP:NT], ACT.Exp).then_inc(ev["w_sample"], 1)
                act.wait_ge(*ev.at("kk_sum", h + 1))
                sc.activation(ch3(T[:, 1, :]), dense[0], ACT.Sqrt).then_inc(ev["kk_norm"], 1)

            with act.Fori(0, NC) as c:
                act.wait_ge(*ev.at("pre_done", HP))
                act.wait_ge(*ev.at("ck_zeroed", 1))
                act.wait_ge(*ev.at("ck_state", c))
                settle(nc.scalar)
                sc.activation(Pb[:, :, 1:65], CUM[:, :, ds(c * C, C)], ACT.Exp).then_inc(ev["ck_p"], 1)
                sc.activation(Pinv, CUM[:, :, ds(c * C, C)], ACT.Exp, scale=-1.0).then_inc(ev["ck_p"], 1)
                act.wait_ge(*ev.at("ck_tok", c + 1))
                sc.activation(vts, ps4(7), ACT.Copy).then_inc(ev["ck_tok_moved"], 1)
                sc.activation(vtok, ps4(5, 0, 128), ACT.Copy).then_inc(ev["ck_tok_moved"], 1)
                sc.activation(btok, ps4(3, 0, 128), ACT.Copy).then_inc(ev["ck_tok_moved"], 1)
                sc.activation(ktok, ps4(4, 0, 128), ACT.Copy).then_inc(ev["ck_tok_moved"], 1)
                act.wait_ge(*ev.at("ck_r", c + 1))
                sc.activation(Rs, ps4(6), ACT.Copy).then_inc(ev["ck_r_moved"], 1)
                for l in range(LEVELS):
                    act.wait_ge(*ev.at("ck_t1", c * LEVELS + (l + 1)))
                    q = halves[1]
                    if l < LEVELS - 1:
                        sc.activation(T1s[q], ps4(0)[q], ACT.Copy)
                    sc.activation(T1d[q, :, q], ps4(0)[q], ACT.Copy).then_inc(ev["ck_t1_act"], 1)
                act.wait_ge(*ev.at("ck_u", c + 1))
                q = halves[1]
                sc.activation(Us[q], ps4(5)[q], ACT.Copy)
                sc.activation(Ud[q, :, q], ps4(5)[q], ACT.Copy).then_inc(ev["ck_u_act"], 1)
                act.wait_ge(*ev.at("ck_y", c + 1))
                settle(nc.scalar)
                sc.activation(CUM[:, :, ds(c * C, C)], ps4(6), ACT.Copy).then_inc(ev["ck_y_out"], 1)

            for h in range(HP):
                act.wait_ge(*ev.at("y_centred", h + 1))
                sc.activation(T[:, 1, :], T[:, 0, :], ACT.Square).then_inc(ev["y_sq"], 1)
                act.wait_ge(*ev.at("y_var", h + 1))
                sc.activation(rstd, rstd, ACT.Sqrt).then_inc(ev["y_root"], 1)
                act.wait_ge(*ev.at("y_final", h + 1))
                sc.activation(YA[0][:, h, :], T[:, 0, :], ACT.Copy).then_inc(ev["ya_high"], 1)
            act.wait_ge(*ev.at("ya_split", HP))
            act.wait_ge(*ev.at("state_stored", 16 * HP * NS))
            act.wait_ge(*ev.at("wkv_stored", 32))
            for h in range(HP):
                sc.activation(YB[0][:, h, :], Q[:, h, :], ACT.Copy).then_inc(ev["yb_high"], 1)

            split(0, AT_MERGE)

            def merge(i, end):
                for s in range(2):
                    split(1 - s, i + (AT_MERGE + s))
                    act.wait_ge(*ev.at("merge_full", i * 2 + (s + 1)))
                    settle(nc.scalar)
                    sc.activation(flat(M[0][:, ds(i * 2 + s, 1), :]), T[:, 0, :], ACT.Copy).then_inc(ev["merge_high"], 1)
            loop(act, KT // 2, merge)

            def out(i, end):
                split(1, i + AT_OUT)
                split(0, i + (AT_OUT + 1))
            loop(act, KT // 2, out)
            norm(2)
            ffn(AT_FFN2, FT, True)
            norm(3, False)
            for t in range(1, 9, 2):
                act.wait_ge(*ev.at("y_trans", t + 1))
                if t >= 3:
                    act.wait_ge(*ev.at("y_stored1", 16 * (t // 2)))
                sc.activation(yout[1], PSf[:, 1024:2048], ACT.Copy).then_inc(ev["y_moved1"], 1)

        @block.vector
        def _(dve):
            ev.prime(dve, "vector")
            v = nc.vector

            def in_turn(instruction):
                dve.drain()

            def split(s, c):
                dve.wait_ge(*ev.at(f"w_high{s}", c + 1))
                in_turn(v.tensor_tensor(wlo[s], stg[s], whi[s].bitcast(F32), ALU.subtract).then_inc(ev[f"w_split{s}"], 1))

            in_turn(v.memset(idle, 0.0))
            dve.wait_ge(*ev.at("par_trans", 1))
            in_turn(v.tensor_copy(par, PS[:, 7, 0:NROWS]).then_inc(ev["par_moved"], 1))
            in_turn(v.tensor_copy(zshift, PS[:, 7, P:P + NS * ZT].rearrange("p (b m) -> p b m", m=ZT)).then_inc(ev["par_moved"], 1))
            dve.wait_ge(*ev.at("par_moved", 2))
            in_turn(v.tensor_scalar(param("da_subln", 0, HP), param("da_subln", 0, HP), 1.0 - LAM_INIT, None, ALU.mult))
            in_turn(v.tensor_scalar(small[:, 32:36], param("rw_k_a", 0, HP), -1.0, 1.0, ALU.mult, ALU.add))
            in_turn(v.tensor_tensor(small[:, 2:3], param("lambda", 0), param("lambda", 1), ALU.mult).then_inc(ev["lam_prod"], 1))
            for k in range(0, KT, 2):
                dve.wait_ge(*ev.at("x_trans", k + 1))
                in_turn(v.tensor_copy(X[:, k, :], PSf[:, 0:NT]).then_inc(ev["x_moved0"], 1))
            dve.wait_ge(*ev.at("x_moved0", KT // 2))
            dve.wait_ge(*ev.at("x_moved1", KT // 2))
            in_turn(v.tensor_copy(small[:, 62:63], param("lambda", 0)).then_inc(ev["x_done"], 1))

            def norm(n, split_h=True):
                name = ("ffn1_norm", "mix_norm", "ffn2_norm", "final_norm")[n]
                dve.wait_ge(*ev.at("sq_used", (n + 1) * KT))
                in_turn(v.tensor_scalar(ch3(rstd), dense[0], 1.0 / D, EPS, ALU.mult, ALU.add).then_inc(ev["mean_made"], 1))
                dve.wait_ge(*ev.at("root_made", n + 1))
                in_turn(v.reciprocal(rstd, rstd))

                def low(k):
                    dve.wait_ge(*ev.at("h_high", n * KT + k + 1))
                    in_turn(v.tensor_tensor(H[1][:, k, :], T[:, k % 2, :], H[0][:, k, :].bitcast(F32), ALU.subtract)\
                        .then_inc(ev["h_ready"], 1))
                for k in range(KT):
                    dst = T[:, k % 2, :] if split_h else X[:, k, :]
                    in_turn(v.scalar_tensor_tensor(dst, X[:, k, :], param(name, k), rstd, ALU.mult, ALU.mult)\
                        .then_inc(ev["h_full"], 1))
                    if split_h and k:
                        low(k - 1)
                if split_h:
                    low(KT - 1)

            def ffn(first, pairs, last):
                for gi, (j0, n) in enumerate(GROUPS):
                    def up(i, end):
                        c = i + first
                        split(1, c)
                        split(0, c + 1)
                        dve.wait_ge(*ev.at("psum_free0", c + 1))
                        dve.wait_ge(*ev.at("unit_done1", c + 1))
                        in_turn(v.tensor_tensor(ch3(T[:, 1, :]), ch3(T[:, 0, :]), dense[1], ALU.mult)\
                            .then_inc(ev["ff_full"], 1))
                        dve.wait_ge(*ev.at("ff_high", i + (pairs + 1)))
                        in_turn(v.tensor_tensor(flat(G[1][:, ds(i, 1), :]), T[:, 1, :],
                                        flat(G[0][:, ds(i, 1), :]).bitcast(F32), ALU.subtract)\
                            .then_inc(ev["psum_free1"], 1))
                    loop(dve, n, up, False)
                    first += n
                    pairs += n

                    def down(i, end):
                        for s in range(2):
                            if s == 0 or not end:
                                split(1 - s, i + (first + s))
                            dve.wait_ge(*ev.at(f"unit_done{s}", i + (first + 1)))
                            xm = flat(X[:, ds(i * 2 + s, 1), :])
                            in_turn(v.scalar_tensor_tensor(ch3(xm), dense[s], 0.5, ch3(xm), ALU.mult, ALU.add)\
                                .then_inc(ev[f"psum_free{s}"], 1))
                    loop(dve, KT // 2, down, last and gi == len(GROUPS) - 1)
                    first += KT // 2
                dve.wait_ge(*ev.at("psum_free0", first))
                dve.wait_ge(*ev.at("psum_free1", first))
                in_turn(v.tensor_copy(small[:, 62:63], param("lambda", 0)).then_inc(ev["x_done"], 1))

            norm(0)
            split(0, 0)
            ffn(0, 0, False)
            norm(1)

            dve.wait_ge(*ev.at("rotary_loaded", 16))
            dve.wait_ge(*ev.at("x_saved", 16))

            def qk(dst, pair):
                def rope(i, end):
                    for s in range(2):
                        split(1 - s, i + (AT_QK + pair + s))
                        dve.wait_ge(*ev.at(f"unit_done{s}", i + (AT_QK + pair + 1)))
                        for b in range(4):
                            src, to = slice(32 * b, 32 * b + 32), slice(32 * (b ^ 1), 32 * (b ^ 1) + 32)
                            in_turn(v.tensor_tensor(ch3(T[to, s, :]), dense[s][src], ch3(rot[src, 1, :]), ALU.mult))
                        o = flat(dst[:, ds(i * 2 + s, 1), :])
                        in_turn(v.tensor_tensor(ch3(o), dense[s], ch3(rot[:, 0, :]), ALU.mult).then_inc(ev[f"psum_free{s}"], 1))
                        dve.wait_ge(*ev.at(f"psum_free{s}", i + (AT_QK + pair + 1)))
                        in_turn(v.tensor_tensor(o, o, T[:, s, :], ALU.add).then_inc(ev["rope_done"], 1))
                loop(dve, HP // 2, rope, False)
            qk(Q, 0)
            qk(Kr, HP // 2)

            def values(i, end):
                split(1, i + AT_V)
                split(0, i + (AT_V + 1))
            loop(dve, HP // 2, values, False)

            def gates(i, end):
                split(1, i + AT_GATES)
                if not end:
                    split(0, i + (AT_GATES + 1))
            loop(dve, GT // 2, gates, True)

            dve.wait_ge(*ev.at("lam_exp", 1))
            in_turn(v.scalar_tensor_tensor(small[:, 3:4], small[:, 0:1], LAM_INIT, small[:, 1:2], ALU.add, ALU.subtract))
            for t in range(9):
                n = P if t < 8 else NS
                dve.wait_ge(*ev.at("v_trans", t + 1))
                dst = Vtok[:, t, :] if t < 8 else wT[1][:, 0:512]
                in_turn(v.tensor_copy(dst[0:n, :], PS[0:n, t % 2, :]).then_inc(ev["v_tok_made"], 1))

            for step in range(8 * HP):
                qi, s = step // HP, step % 2
                n = (qi + 1) * P
                scores = PSf[:, 0:2048].rearrange("p (m n) -> p m n", m=2)
                dve.wait_ge(*ev.at("scores_done", step + 1))
                diag = scores[:, :, qi * P:n]
                in_turn(v.tensor_tensor(diag, diag, K("causal").unsqueeze(1).broadcast_to([P, 2, P]), ALU.add))
                top = small[:, 24 + 2 * s:26 + 2 * s]
                in_turn(v.tensor_reduce(top, scores[:, :, 0:n], AX, ALU.max))
                in_turn(v.tensor_scalar(small[:, 16 + 4 * s:18 + 4 * s], top, -SCALE, None, ALU.mult).then_inc(ev["neg_max"], 1))
                dve.wait_ge(*ev.at("probs_made", 2 * step + 2))
                inv = small[:, 28 + 2 * s:30 + 2 * s]
                in_turn(v.reciprocal(inv, small[:, 18 + 4 * s:20 + 4 * s]))
                in_turn(v.tensor_tensor(inv[:, 1:2], inv[:, 1:2], small[:, 3:4], ALU.mult))
                p2 = pr[:, s, 1, 0:n]
                in_turn(v.tensor_scalar(p2, p2, inv[:, 1:2], None, ALU.mult))
                p1 = pr[:, s, 0, 0:n]
                in_turn(v.scalar_tensor_tensor(p1, p1, inv[:, 0:1], p2, ALU.mult, ALU.subtract).then_inc(ev["w_ready"], 1))
                if qi >= 4:
                    dve.wait_ge(*ev.at("w_trans_hi", step + 1 - 4 * HP))
                    in_turn(v.tensor_copy(wT[s][:, 512:n], PS[:, 5, 0:n - 512]).then_inc(ev["w_hi_moved"], 1))

            dve.wait_ge(*ev.at("o_moved", 8 * HP))
            dve.wait_ge(*ev.at("v_tok_made", 9))
            in_turn(v.tensor_copy(vsam, Vt[:, :, NP:NT]))
            qk3 = qk_cols.rearrange("p (h b) -> p h b", b=NS)
            in_turn(v.tensor_tensor(qk3, Q[:, :, NP:NT], Kr[:, :, NP:NT], ALU.mult).then_inc(ev["s_self_prod"], 1))
            dve.wait_ge(*ev.at("s_self", 1))
            for a in range(2):
                in_turn(v.tensor_copy(sself.rearrange("p (b h a) -> p a h b", h=HP, a=2)[:, a],
                              PS[:, 7, 32 * a:32 * a + 32].rearrange("p (h b) -> p h b", b=NS)).then_inc(ev["s_self_moved"], 1))
            with dve.Fori(0, NS) as b:
                in_turn(v.tensor_tensor(Qdg.rearrange("p (h n) -> p h n", h=HP), over_heads(K("ident")),
                                bc(Q[:, :, ds(b + NP, 1)], P), ALU.mult).then_inc(ev["q_diag"], 1))
                dve.wait_ge(*ev.at("q_bc", b + 1))
                for g in range(4):
                    dve.wait_ge(*ev.at(f"page_loaded{g}", b * 64 + 64))
                    in_turn(v.tensor_tensor(prod.rearrange("p (j n) -> p j n", j=4), ring[:, g],
                                    Qbc.unsqueeze(1).broadcast_to([P, 4, 512]), ALU.mult).then_inc(ev[f"k_used{g}"], 1))
                    dve.wait_ge(*ev.at(f"k_used{g}", b + 1))
                    in_turn(v.tensor_reduce(SC[:, ds(b * 128 + 32 * g, 32)], prod.rearrange("p (a d) -> p a d", d=64), AX,
                                    ALU.add))
            smx = smaxp.rearrange("p (b m) -> p b m", b=NS)
            in_turn(v.tensor_reduce(smx, SC.rearrange("p (b g m) -> p b m g", b=NS, g=PAGES), AX, ALU.max)\
                .then_inc(ev["s_max_part"], 1))
            dve.wait_ge(*ev.at("s_max_all", 1))
            dve.wait_ge(*ev.at("s_self_moved", 2))
            in_turn(v.tensor_tensor(smax, smax, sself, ALU.max))

            def pages(a):
                return a.rearrange("p (b m) -> p b m", b=NS).unsqueeze(2).broadcast_to([P, NS, PAGES, 2 * HP])
            in_turn(v.tensor_tensor(VIEW_SC, VIEW_SC, pages(smax), ALU.subtract).then_inc(ev["s_shifted"], 1))
            in_turn(v.tensor_tensor(sself, sself, smax, ALU.subtract).then_inc(ev["s_shifted"], 1))
            dve.wait_ge(*ev.at("s_exp", 2))
            in_turn(v.tensor_reduce(smx, SC.rearrange("p (b g m) -> p b m g", b=NS, g=PAGES), AX, ALU.add)\
                .then_inc(ev["s_sum_part"], 1))
            dve.wait_ge(*ev.at("s_sum", 1))
            in_turn(v.tensor_tensor(ssum, sexp, PS[:, 7, 0:64], ALU.add))
            in_turn(v.reciprocal(ssum, ssum))
            odd = ssum.rearrange("p (n a) -> p a n", a=2)[:, 1]
            in_turn(v.tensor_scalar(odd, odd, small[:, 3:4], None, ALU.mult))
            in_turn(v.tensor_tensor(VIEW_SC, VIEW_SC, pages(ssum), ALU.mult))
            in_turn(v.tensor_tensor(sexp, sexp, ssum, ALU.mult))
            two = SC.rearrange("p (n a) -> p a n", a=2)
            in_turn(v.tensor_tensor(Wp, two[:, 0], two[:, 1], ALU.subtract).then_inc(ev["s_weights"], 1))
            two = sexp.rearrange("p (n a) -> p a n", a=2)
            in_turn(v.tensor_tensor(wself, two[:, 0], two[:, 1], ALU.subtract).then_inc(ev["s_weights"], 1))
            dve.wait_ge(*ev.at("s_weights", 2))
            with dve.Fori(0, NS // 2) as i:
                for q in range(2):
                    b = i * 2 + q
                    in_turn(v.tensor_tensor(vw.unsqueeze(2), vsam[:, :, ds(b, 1)],
                                    wself.rearrange("p (b h) -> p h b", b=NS)[:, :, ds(b, 1)], ALU.mult))
                    dve.wait_ge(*ev.at("v_used3", b + 1))
                    in_turn(v.tensor_tensor(Q[:, :, ds(b + NP, 1)], PS[:, 4 * q:4 * q + 4, 0:1], vw.unsqueeze(2), ALU.add)\
                        .then_inc(ev["o_sample"], 1))

            for h in range(HP):
                dve.wait_ge(*ev.at("o_sq_sum", h + 1))
                in_turn(v.tensor_scalar(ch3(rstd), dense[0], 1.0 / P, EPS, ALU.mult, ALU.add).then_inc(ev["o_mean"], 1))
                dve.wait_ge(*ev.at("o_root", h + 1))
                in_turn(v.reciprocal(rstd, rstd))
                in_turn(v.scalar_tensor_tensor(Q[:, h, :], Q[:, h, :], param("da_subln", h), rstd, ALU.mult, ALU.mult)\
                    .then_inc(ev["yb_done"], 1))

            split(0, AT_Z)

            def z_mix(i, end):
                for s in range(2):
                    if s == 0 or not end:
                        split(1 - s, i + (AT_Z + s))
                    m = i * 2 + s
                    dve.wait_ge(*ev.at(f"psum_free{s}", i + (AT_Z + 1)))
                    zm = flat(Z[:, ds(m, 1), :])
                    z = T[:, s, :]
                    in_turn(v.tensor_copy(zlast[:, :, ds(m, 1)], z[:, NP - 1:NT].unsqueeze(2)).then_inc(ev["z_last"], 1))
                    in_turn(v.tensor_tensor(zm[:, 1:NP], z[:, 0:NP - 1], z[:, 1:NP], ALU.subtract))
                    in_turn(v.tensor_scalar(zm[:, 0:1], z[:, 0:1], -1.0, None, ALU.mult))
                    in_turn(v.tensor_tensor(zm[:, NP:NT], zshift[:, :, ds(m, 1)].rearrange("p b a -> p (b a)"), z[:, NP:NT],
                                    ALU.subtract))
                    in_turn(v.scalar_tensor_tensor(zm, zm, par[:, ds(m + ROW["rw_mu"], 1)], z, ALU.mult, ALU.add)\
                        .then_inc(ev[f"z_mixed{s}"], 1))
            loop(dve, ZT // 2, z_mix, True)
            dve.wait_ge(*ev.at("z_rows_trans", 1))
            in_turn(v.tensor_copy(zrow[0:9 * ZT, :], PS[0:9 * ZT, 7, 0:P]).then_inc(ev["z_rows_made"], 1))
            dve.wait_ge(*ev.at("z_mixed0", ZT // 2))
            dve.wait_ge(*ev.at("z_mixed1", ZT // 2))
            dve.wait_ge(*ev.at("lora_loaded", 48))

            for h in range(HP):
                dve.wait_ge(*ev.at("pre_done", h))
                in_turn(v.tensor_scalar(KKn[:, h, :], Kf[:, h, :], param("rw_k_k", h), None, ALU.mult).then_inc(ev["kk_scaled"], 1))
                dve.wait_ge(*ev.at("lora_act", 2 * h + 2))
                ld = T[:, 0, :]
                in_turn(v.tensor_scalar(ld, ld, LOGDECAY, None, ALU.mult).then_inc(ev["ld_made"], 1))
                dve.wait_ge(*ev.at("ld_made", h + 1))
                in_turn(v.tensor_tensor_scan(CUM[:, h, 0:NP], fresh, ld[:, 0:NP], 0.0, ALU.mult, ALU.add))
                dve.wait_ge(*ev.at("kk_norm", h + 1))
                dve.wait_ge(*ev.at("kk_scaled", h + 1))
                nrm = T[:, 1, :]
                in_turn(v.tensor_scalar(nrm, nrm, 1e-12, None, ALU.max))
                in_turn(v.reciprocal(nrm, nrm))
                in_turn(v.tensor_tensor(KKn[:, h, :], KKn[:, h, :], nrm, ALU.mult))
                in_turn(v.tensor_scalar(nrm, Bf[:, h, :], param("rw_k_a", h), small[:, 32 + h:33 + h], ALU.mult, ALU.add))
                in_turn(v.tensor_tensor(Kf[:, h, :], Kf[:, h, :], nrm, ALU.mult))
                in_turn(v.tensor_tensor(Bf[:, h, :], Bf[:, h, :], KKn[:, h, :], ALU.mult))
                dve.wait_ge(*ev.at("w_sample", h + 1))
                in_turn(v.tensor_copy(small[:, 62:63], param("lambda", 0)).then_inc(ev["pre_done"], 1))

            dve.wait_ge(*ev.at("z_stored", 32))
            in_turn(v.memset(wk[:, bd_first:bd_last], 0.0))
            in_turn(v.memset(T[:, 0, 0:768], 0.0))
            in_turn(v.memset(Pb[:, :, 0:1], 1.0))
            in_turn(v.tensor_copy(small[:, 62:63], param("lambda", 0)).then_inc(ev["ck_zeroed"], 1))

            with dve.Fori(0, NC) as c:
                now = ds(c * C, C)
                dve.wait_ge(*ev.at("ck_p", c * 2 + 2))
                in_turn(v.scalar_tensor_tensor(ar[:, :, 0, :], KKn[:, :, now], -1.0, Pb[:, :, 0:64], ALU.mult, ALU.mult)\
                    .then_inc(ev["ck_at"], 1))
                in_turn(v.tensor_tensor(bts, Bf[:, :, now], Pinv, ALU.mult).then_inc(ev["ck_bt"], 1))
                in_turn(v.tensor_tensor(kts, Kf[:, :, now], Pinv, ALU.mult).then_inc(ev["ck_kt"], 1))
                in_turn(v.tensor_tensor(ar[:, :, 1, :], Rf[:, :, now], Pb[:, :, 1:65], ALU.mult).then_inc(ev["ck_rt"], 1))
                dve.wait_ge(*ev.at("ck_gram", c + 1))
                strict, incl = over_heads(K("strict_st")), over_heads(K("incl_st"))
                ab, ak = ps4(0, 0, 128), ps4(1, 0, 128)
                in_turn(v.tensor_tensor(LTs, ab[:, :, 0:64], strict, ALU.mult))
                in_turn(v.tensor_tensor(Xs, ps4(2), over_heads(K("pair_ts")), ALU.mult))
                in_turn(v.tensor_tensor(Ys, LTs, over_heads(K("pair_st")), ALU.mult))
                in_turn(v.tensor_tensor(Xs, Xs, over_heads(K("ident_stack")), ALU.add).then_inc(ev["ck_x"], 1))
                for q in halves:
                    in_turn(v.tensor_tensor(aakd[q, :, q], ak[q, :, 0:64], strict[q], ALU.mult).then_inc(ev["ck_aak"], 1))
                in_turn(v.tensor_tensor(Ys, Ys, over_heads(K("ident_stack")), ALU.add))
                in_turn(v.tensor_tensor(arbs, ab[:, :, 64:128], incl, ALU.mult).then_inc(ev["ck_ar"], 1))
                in_turn(v.tensor_tensor(arks, ak[:, :, 64:128], incl, ALU.mult).then_inc(ev["ck_ar"], 1))
                for q in halves:
                    in_turn(v.tensor_copy(Yd[q, :, q], Ys[q]))
                for q in halves:
                    in_turn(v.tensor_tensor(btmd[0][q, :, q], LTs[q], over_heads(K("level0"))[q], ALU.mult)\
                        .then_inc(ev["ck_level"], 1))
                for l in range(LEVELS):
                    q = halves[0]
                    dve.wait_ge(*ev.at("ck_t1", c * LEVELS + (l + 1)))
                    if l < LEVELS - 1:
                        in_turn(v.tensor_copy(T1s[q], ps4(0)[q]))
                    in_turn(v.tensor_copy(T1d[q, :, q], ps4(0)[q]).then_inc(ev["ck_t1_dve"], 1))
                    if l < LEVELS - 1:
                        for q in halves:
                            in_turn(v.tensor_tensor(btmd[(l + 1) % 2][q, :, q], LTs[q], over_heads(K(f"level{l + 1}"))[q], ALU.mult))
                    dve.wait_ge(*ev.at("ck_d", c * LEVELS + (l + 1)))
                    if l < LEVELS - 1:
                        in_turn(v.tensor_tensor(Xs, Xs, ps4(1), ALU.add))
                    in_turn(v.tensor_tensor(Ys, Ys, ps4(1, 256), ALU.add))
                    for q in halves:
                        in_turn(v.tensor_copy(Yd[q, :, q], Ys[q]).then_inc(ev["ck_level"], 1))
                dve.wait_ge(*ev.at("ck_u", c + 1))
                q = halves[0]
                in_turn(v.tensor_copy(Us[q], ps4(5)[q]).then_inc(ev["ck_u_dve"], 1))
                in_turn(v.tensor_copy(Ud[q, :, q], ps4(5)[q]).then_inc(ev["ck_u_dve"], 1))
                dve.wait_ge(*ev.at("ck_y", c + 1))
                in_turn(v.tensor_tensor(Ss, Ss, ps4(7), ALU.add))
                in_turn(v.tensor_tensor(Ss, Ss, bc(Pb[:, :, 64:65], 64), ALU.mult))
                in_turn(v.tensor_copy(Sd[0:64, :, 0:64], Ss[0:64]))
                in_turn(v.tensor_copy(Sd[64:128, :, 64:128], Ss[64:128]).then_inc(ev["ck_state"], 1))

            dve.wait_ge(*ev.at("wkv_trans", 1))
            for q in halves:
                in_turn(v.tensor_copy(wfin[q], ps4(0, 0, 128)[q, :, q]).then_inc(ev["wkv_made"], 1))

            dve.wait_ge(*ev.at("state_loaded", 16 * HP * NS))
            for h in range(HP):
                for n, vec in enumerate((KKn[:, h, NP:NT], wsam[:, h, :], Bf[:, h, NP:NT], Kf[:, h, NP:NT], Rf[:, h, NP:NT])):
                    in_turn(v.tensor_tensor(dg[:, n], K("ident_stack").unsqueeze(1).broadcast_to([P, NS, 64]),
                                    vec.unsqueeze(2).broadcast_to([P, NS, 64]), ALU.mult).then_inc(ev["row_diag"], 1))
                dve.wait_ge(*ev.at("rows_made", h + 1))
                row = [PS[:, n, :].rearrange("p (b j) -> p b j", b=NS) for n in range(5)]
                S = St[:, h]
                in_turn(v.tensor_tensor(stm, S, row[0], ALU.mult))
                in_turn(v.tensor_reduce(sa, stm, AX, ALU.add))
                in_turn(v.tensor_tensor(S, S, row[1], ALU.mult))
                in_turn(v.tensor_tensor(stm, sa.unsqueeze(2).broadcast_to([P, NS, 64]), row[2], ALU.mult))
                in_turn(v.tensor_tensor(S, S, stm, ALU.subtract))
                in_turn(v.tensor_tensor(stm, Vf[:, h, NP:NT].unsqueeze(2).broadcast_to([P, NS, 64]), row[3], ALU.mult))
                in_turn(v.tensor_tensor(S, S, stm, ALU.add))
                in_turn(v.tensor_tensor(stm, S, row[4], ALU.mult))
                in_turn(v.tensor_reduce(CUM[:, h, NP:NT], stm, AX, ALU.add))
                in_turn(v.tensor_copy(small[:, 62:63], param("lambda", 0)).then_inc(ev["state_new"], 1))

            for h in range(HP):
                y, t0, t1 = CUM[:, h, :], T[:, 0, :], T[:, 1, :]
                dve.wait_ge(*ev.at("y_sum", h + 1))
                dve.wait_ge(*ev.at("ya_high", h))
                in_turn(v.scalar_tensor_tensor(ch3(t0), dense[0], -1.0 / 64, ch3(y), ALU.mult, ALU.add).then_inc(ev["y_centred"], 1))
                dve.wait_ge(*ev.at("y_sq_sum", h + 1))
                in_turn(v.tensor_scalar(ch3(rstd), dense[1], 1.0 / 64, GN_EPS, ALU.mult, ALU.add).then_inc(ev["y_var"], 1))
                in_turn(v.scalar_tensor_tensor(t1, Rf[:, h, :], param("rw_r_k", h), Kf[:, h, :], ALU.mult, ALU.mult)\
                    .then_inc(ev["bonus_prod"], 1))
                dve.wait_ge(*ev.at("y_root", h + 1))
                in_turn(v.reciprocal(rstd, rstd))
                in_turn(v.scalar_tensor_tensor(t0, t0, param("rw_ln_w", h), rstd, ALU.mult, ALU.mult))
                dve.wait_ge(*ev.at("bonus_sum", h + 1))
                in_turn(v.tensor_tensor(ch3(t1), ch3(Vf[:, h, :]), dense[0], ALU.mult))
                in_turn(v.scalar_tensor_tensor(t0, t0, param("rw_ln_b", h), t1, ALU.add, ALU.add))
                dve.wait_ge(*ev.at("g_made", h + 1))
                in_turn(v.tensor_tensor(ch3(t0), ch3(t0), dense[1], ALU.mult).then_inc(ev["y_final"], 1))
                dve.wait_ge(*ev.at("ya_high", h + 1))
                in_turn(v.tensor_tensor(YA[1][:, h, :], t0, YA[0][:, h, :].bitcast(F32), ALU.subtract).then_inc(ev["ya_split"], 1))
                in_turn(v.tensor_copy(small[:, 62:63], param("lambda", 0)))
                in_turn(v.tensor_copy(small[:, 63:64], param("lambda", 0)))
            for h in range(HP):
                dve.wait_ge(*ev.at("yb_high", h + 1))
                in_turn(v.tensor_tensor(YB[1][:, h, :], Q[:, h, :], YB[0][:, h, :].bitcast(F32), ALU.subtract)\
                    .then_inc(ev["yb_split"], 1))

            split(0, AT_MERGE)

            def merge(i, end):
                for s in range(2):
                    split(1 - s, i + (AT_MERGE + s))
                    dve.wait_ge(*ev.at(f"unit_done{s}", i + (AT_MERGE + 1)))
                    dve.wait_ge(*ev.at(f"gates_back{s}", i * 32 + 32))
                    m = i * 2 + s
                    ga, gb = gring[:, s, 0, :], gring[:, s, 1, :]
                    dve.wait_ge(*ev.at("merge_high", m))
                    in_turn(v.tensor_tensor(ch3(T[:, 0, :]), ch3(ga), dense[0], ALU.mult))
                    in_turn(v.tensor_tensor(ch3(T[:, 1, :]), ch3(gb), dense[1], ALU.mult).then_inc(ev[f"psum_free{s}"], 1))
                    dve.wait_ge(*ev.at(f"psum_free{s}", i + (AT_MERGE + 1)))
                    in_turn(v.tensor_tensor(T[:, 0, :], T[:, 0, :], T[:, 1, :], ALU.add).then_inc(ev["merge_full"], 1))
                    dve.wait_ge(*ev.at("merge_high", m + 1))
                    in_turn(v.tensor_tensor(flat(M[1][:, ds(m, 1), :]), T[:, 0, :], flat(M[0][:, ds(m, 1), :]).bitcast(F32),
                                    ALU.subtract).then_inc(ev["merged"], 1))
            loop(dve, KT // 2, merge, False)
            dve.wait_ge(*ev.at("x_back", 16))

            def out(i, end):
                for s in range(2):
                    split(1 - s, i + (AT_OUT + s))
                    dve.wait_ge(*ev.at(f"unit_done{s}", i + (AT_OUT + 1)))
                    xm = flat(X[:, ds(i * 2 + s, 1), :])
                    in_turn(v.tensor_tensor(ch3(xm), ch3(xm), dense[s], ALU.add).then_inc(ev[f"psum_free{s}"], 1))
            loop(dve, KT // 2, out, False)
            dve.wait_ge(*ev.at("psum_free0", AT_FFN2))
            dve.wait_ge(*ev.at("psum_free1", AT_FFN2))
            in_turn(v.tensor_copy(small[:, 62:63], param("lambda", 0)).then_inc(ev["x_done"], 1))
            norm(2)
            ffn(AT_FFN2, FT, True)
            norm(3, False)
            for t in range(0, 9, 2):
                n = P if t < 8 else NS
                dve.wait_ge(*ev.at("y_trans", t + 1))
                if t >= 2:
                    dve.wait_ge(*ev.at("y_stored0", 16 * (t // 2)))
                in_turn(v.tensor_copy(yout[0][0:n, :], PSf[0:n, 0:1024]).then_inc(ev["y_moved0"], 1))

        @block.tensor
        def _(pe):
            ev.prime(pe, "tensor")
            mm = nc.tensor.matmul

            def product(s, R, nk, k0=0, w0=0):
                for k in range(nk):
                    for n, (w, r) in enumerate(((whi, R[0]), (whi, R[1]), (wlo, R[0]))):
                        for j in range(NCH):
                            last = mm(dense[s][:, j], w[w0][:, k0 + k, :], r[:, k, j * CH:(j + 1) * CH],
                                      start=(k == 0 and n == 0), stop=(k == nk - 1 and n == 2))
                return last

            def unit(s, c, R, nk=KT):
                pe.wait_ge(*ev.at(f"w_split{s}", c + 1))
                pe.wait_ge(*ev.at(f"psum_free{s}", c))
                product(s, R, nk, 0, s).then_inc(ev[f"unit_done{s}"], 1)

            def column_sums(s, what, src):
                for j in range(NCH):
                    last = mm(dense[s][:, j], what, src[:, j * CH:(j + 1) * CH], start=True, stop=True)
                return last

            pe.wait_ge(*ev.at("params_loaded", 16 * (len(PARAMS) + 6)))
            nc.tensor.transpose(PS[:, 7, 0:NROWS], prow[0:NROWS, :], K("ident")[0:NROWS, 0:NROWS])
            nc.tensor.transpose(PS[:, 7, P:P + NS * ZT], srow[0:NS * ZT, :], K("ident")[0:NS * ZT, 0:NS * ZT])\
                .then_inc(ev["par_trans"], 1)
            pe.wait_ge(*ev.at("x_loaded", 16 * 9))
            for k in range(KT):
                base = 1536 * (k % 2)
                if k >= 2:
                    pe.wait_ge(*ev.at(f"x_moved{k % 2}", k // 2))
                for t in range(8):
                    nc.tensor.transpose(PSf[:, base + t * P:base + (t + 1) * P], xin[:, t, k * P:(k + 1) * P], K("ident"))
                nc.tensor.transpose(PSf[:, base + NP:base + NT], xin[0:NS, 8, k * P:(k + 1) * P], K("ident")[0:NS, 0:NS])\
                    .then_inc(ev["x_trans"], 1)

            def norm(n):
                for k in range(KT):
                    pe.wait_ge(*ev.at("sq_made", n * KT + k + 1))
                    for j in range(NCH):
                        last = mm(dense[0][:, j], K("ones"), T[:, k % 2, j * CH:(j + 1) * CH],
                                  start=(k == 0), stop=(k == KT - 1))
                    last.then_inc(ev["sq_used"], 1)

            def ffn(first, last):
                for gi, (j0, n) in enumerate(GROUPS):
                    def up(i, end):
                        for s in range(2):
                            unit(s, i + first, H)
                    loop(pe, n, up)
                    first += n
                    pe.wait_ge(*ev.at("psum_free1", first))

                    def down(i, end):
                        for s in range(2):
                            unit(s, i + first, G, n)
                    loop(pe, KT // 2, down)
                    first += KT // 2

            norm(0)
            pe.wait_ge(*ev.at("h_ready", KT))
            ffn(0, False)
            norm(1)
            pe.wait_ge(*ev.at("h_ready", 2 * KT))

            def units(first, n, R):
                def body(i, end):
                    for s in range(2):
                        unit(s, i + first, R)
                loop(pe, n // 2, body)
            units(AT_QK, 3 * HP + GT, H)

            pe.wait_ge(*ev.at("lam_prod", 1))
            mm(PS[:, 7, 0:1], K("top_ones"), small[:, 2:3], start=True, stop=True)
            mm(PS[:, 7, 1:2], K("bottom_ones"), small[:, 2:3], start=True, stop=True).then_inc(ev["lam_sums"], 1)
            pe.wait_ge(*ev.at("psum_free0", AT_Z))
            pe.wait_ge(*ev.at("psum_free1", AT_Z))
            pe.wait_ge(*ev.at("rope_done", 2 * HP))
            for t in range(9):
                n = P if t < 8 else NS
                if t >= 2:
                    pe.wait_ge(*ev.at("v_tok_made", t - 1))
                    pe.wait_ge(*ev.at("k_tok_made", t - 1))
                for h in range(HP):
                    last = nc.tensor.transpose(PS[0:n, t % 2, h * P:(h + 1) * P], Vt[:, h, t * P:t * P + n], K("ident"))
                last.then_inc(ev["v_trans"], 1)
                for h in range(HP):
                    last = nc.tensor.transpose(PS[0:n, 2 + t % 2, h * P:(h + 1) * P], Kr[:, h, t * P:t * P + n], K("ident"))
                last.then_inc(ev["k_trans"], 1)

            pe.wait_ge(*ev.at("v_tok_made", 9))
            pe.wait_ge(*ev.at("k_tok_made", 9))
            pe.wait_ge(*ev.at("lam_exp", 1))

            def scores(step):
                qi, h = step // HP, step % HP
                n = (qi + 1) * P
                pe.wait_ge(*ev.at("probs_made", 2 * step))
                for m in range(2):
                    q = halves[m]
                    for j in range(0, n, 512):
                        w = min(512, n - j)
                        last = mm(PSf[:, m * 1024 + j:m * 1024 + j + w], Q[q, h, qi * P:n], Kr[q, h, j:j + w],
                                  start=True, stop=True)
                last.then_inc(ev["scores_done"], 1)
            scores(0)
            for step in range(8 * HP):
                qi, h, s = step // HP, step % HP, step % 2
                if step + 1 < 8 * HP:
                    scores(step + 1)
                pe.wait_ge(*ev.at("w_ready", step + 1))
                pe.wait_ge(*ev.at("w_lo_moved", step))
                for t in range(qi + 1):
                    if t == 4 and step > 4 * HP:
                        pe.wait_ge(*ev.at("w_hi_moved", step - 4 * HP))
                    last = nc.tensor.transpose(PS[:, 4 + t // 4, (t % 4) * P:(t % 4 + 1) * P],
                                               pr[:, s, 0, t * P:(t + 1) * P], K("ident"))
                    if t == min(3, qi):
                        last.then_inc(ev["w_trans_lo"], 1)
                    elif t == qi:
                        last.then_inc(ev["w_trans_hi"], 1)
                pe.wait_ge(*ev.at("w_lo_moved", step + 1))
                if qi >= 4:
                    pe.wait_ge(*ev.at("w_hi_moved", step + 1 - 4 * HP))
                if step >= 2:
                    pe.wait_ge(*ev.at("o_moved", step - 1))
                for t in range(qi + 1):
                    last = mm(PS[:, 6 + s, 0:P], Vtok[:, t, h * P:(h + 1) * P], wT[s][:, t * P:(t + 1) * P],
                              start=(t == 0), stop=(t == qi))
                last.then_inc(ev["o_done"], 1)

            pe.wait_ge(*ev.at("o_moved", 8 * HP))
            pe.wait_ge(*ev.at("s_self_prod", 1))
            mm(PS[:, 7, 0:32], K("top_ones"), qk_cols, start=True, stop=True)
            mm(PS[:, 7, 32:64], K("bottom_ones"), qk_cols, start=True, stop=True).then_inc(ev["s_self"], 1)
            with pe.Fori(0, NS) as b:
                pe.wait_ge(*ev.at("q_diag", b + 1))
                pe.wait_ge(*ev.at("q_bc", b))
                mm(PS[:, 6, :], K("ones"), Qdg, start=True, stop=True).then_inc(ev["q_rows"], 1)
            pe.wait_ge(*ev.at("s_self_moved", 2))
            pe.wait_ge(*ev.at("s_sum_part", 1))
            mm(PS[:, 7, 0:64], K("ones"), smaxp, start=True, stop=True).then_inc(ev["s_sum"], 1)
            pe.wait_ge(*ev.at("s_weights", 2))
            pe.wait_ge(*ev.at("q_bc", NS))
            with pe.Fori(0, NS // 2) as i:
                for q in range(2):
                    b = i * 2 + q
                    pe.wait_ge(*ev.at("o_sample", i * 2))
                    for g in range(4):
                        pe.wait_ge(*ev.at(f"page_loaded{g}", b * 64 + (64 * NS + 64)))
                        for j in range(4):
                            for h in range(HP):
                                last = mm(PS[:, 4 * q + h, 0:1], ring[:, g, j, h * P:(h + 1) * P],
                                          VIEW_W[:, ds(b, 1), 4 * g + j, h],
                                          start=(g == 0 and j == 0), stop=(g == 3 and j == 3))
                        last.then_inc(ev[f"v_used{g}"], 1)
            pe.wait_ge(*ev.at("o_sample", NS))
            for h in range(HP):
                pe.wait_ge(*ev.at("o_sq", h + 1))
                if h:
                    pe.wait_ge(*ev.at("o_mean", h))
                column_sums(0, K("ones"), T[:, h % 2, :]).then_inc(ev["o_sq_sum"], 1)
            pe.wait_ge(*ev.at("o_mean", HP))

            units(AT_Z, ZT, H)
            pe.wait_ge(*ev.at("z_last", ZT))
            nc.tensor.transpose(PS[0:9 * ZT, 7, 0:P], flat(zlast), K("ident")).then_inc(ev["z_rows_trans"], 1)
            pe.wait_ge(*ev.at("psum_free0", AT_MERGE))
            pe.wait_ge(*ev.at("psum_free1", AT_MERGE))
            pe.wait_ge(*ev.at("lora_loaded", 48))
            pe.wait_ge(*ev.at("z_act", 2))
            for h in range(HP):
                hh = slice(h * P, (h + 1) * P)
                if h:
                    pe.wait_ge(*ev.at("kk_norm", h))
                    pe.wait_ge(*ev.at("lora_act", 2 * h))
                for q, d in ((halves[0], 0), (halves[1], 1)):
                    for j in range(NCH):
                        last = mm(dense[d][:, j], lw2[q, hh], Z[q, 12, j * CH:(j + 1) * CH], start=True, stop=True)
                last.then_inc(ev["lora_made"], 1)
                pe.wait_ge(*ev.at("kk_sq", h + 1))
                pe.wait_ge(*ev.at("lora_act", 2 * h + 2))
                column_sums(0, K("block_ones"), T[:, 1, :]).then_inc(ev["kk_sum"], 1)
            pe.wait_ge(*ev.at("kk_norm", HP))
            pe.wait_ge(*ev.at("z_rows_made", 1))

            with pe.Fori(0, NC) as c:
                pe.wait_ge(*ev.at("ck_diag", c * 2 + 2))
                pe.wait_ge(*ev.at("ck_rt", c + 1))
                pe.wait_ge(*ev.at("ck_y_out", c))
                for h in range(HP):
                    mm(ps4(0, 0, 128)[:, h], btd[:, h], ar[:, h].rearrange("p a t -> p (a t)"), start=True, stop=True)
                for h in range(HP):
                    mm(ps4(1, 0, 128)[:, h], ktd[:, h], ar[:, h].rearrange("p a t -> p (a t)"), start=True, stop=True)
                for h in range(HP):
                    last = mm(ps4(2)[:, h], atd[:, h], bts[:, h], start=True, stop=True)
                last.then_inc(ev["ck_gram"], 1)
                for h in range(HP):
                    mm(ps4(7)[:, h], vtd[:, h], K("ident_stack"), start=True, stop=True)
                    nc.tensor.transpose(ps4(5, 0, 128)[:, h], vtd[:, h], K("ident"))
                    nc.tensor.transpose(ps4(3, 0, 128)[:, h], btd[:, h], K("ident"))
                    last = nc.tensor.transpose(ps4(4, 0, 128)[:, h], ktd[:, h], K("ident"))
                last.then_inc(ev["ck_tok"], 1)
                pe.wait_ge(*ev.at("ck_aak", c * 2 + 2))
                pe.wait_ge(*ev.at("ck_tok_moved", c * 4 + 1))
                pe.wait_ge(*ev.at("ck_state", c))
                for h in range(HP):
                    mm(ps4(6)[:, h], atd[:, h], Ss[:, h], start=True, stop=False)
                    last = mm(ps4(6)[:, h], aakd[:, h], vts[:, h], start=False, stop=True)
                last.then_inc(ev["ck_r"], 1)
                pe.wait_ge(*ev.at("ck_x", c + 1))
                pe.wait_ge(*ev.at("ck_ar", c * 2 + 2))
                for l in range(LEVELS):
                    pe.wait_ge(*ev.at("ck_level", c * (2 * LEVELS + 2) + (2 * l + 2)))
                    for h in range(HP):
                        last = mm(ps4(0)[:, h], btmd[l % 2][:, h], Xs[:, h], start=True, stop=True)
                    last.then_inc(ev["ck_t1"], 1)
                    pe.wait_ge(*ev.at("ck_t1_act", c * LEVELS + (l + 1)))
                    pe.wait_ge(*ev.at("ck_t1_dve", c * LEVELS + (l + 1)))
                    if l < LEVELS - 1:
                        for h in range(HP):
                            mm(ps4(1)[:, h], Yd[:, h], T1s[:, h], start=True, stop=True)
                    for h in range(HP):
                        last = mm(ps4(1, 256)[:, h], T1d[:, h], Ys[:, h], start=True, stop=True)
                    last.then_inc(ev["ck_d"], 1)
                pe.wait_ge(*ev.at("ck_level", (c + 1) * (2 * LEVELS + 2)))
                pe.wait_ge(*ev.at("ck_r_moved", c + 1))
                pe.wait_ge(*ev.at("ck_tok_moved", c * 4 + 4))
                for h in range(HP):
                    last = mm(ps4(5)[:, h], Yd[:, h], Rs[:, h], start=True, stop=True)
                last.then_inc(ev["ck_u"], 1)
                pe.wait_ge(*ev.at("ck_u_act", c + 1))
                pe.wait_ge(*ev.at("ck_u_dve", c * 2 + 2))
                for h in range(HP):
                    mm(ps4(7)[:, h], btok[:, h], Us[:, h], start=True, stop=False)
                    mm(ps4(7)[:, h], ktok[:, h], vts[:, h], start=False, stop=True)
                for h in range(HP):
                    mm(ps4(6)[:, h], Sd[:, h], ar[:, h, 1, :], start=True, stop=False)
                    mm(ps4(6)[:, h], Ud[:, h], arbs[:, h], start=False, stop=False)
                    last = mm(ps4(6)[:, h], vtok[:, h], arks[:, h], start=False, stop=True)
                last.then_inc(ev["ck_y"], 1)

            pe.wait_ge(*ev.at("ck_state", NC))
            for h in range(HP):
                last = nc.tensor.transpose(ps4(0, 0, 128)[:, h], Sd[:, h], K("ident"))
            last.then_inc(ev["wkv_trans"], 1)
            pe.wait_ge(*ev.at("wkv_made", 2))
            for h in range(HP):
                pe.wait_ge(*ev.at("row_diag", 5 * h + 5))
                if h:
                    pe.wait_ge(*ev.at("state_new", h))
                for n in range(5):
                    last = mm(PS[:, n, :], K("block_ones"), dg[:, n].rearrange("p b j -> p (b j)"), start=True, stop=True)
                last.then_inc(ev["rows_made"], 1)
            pe.wait_ge(*ev.at("state_new", HP))
            pe.wait_ge(*ev.at("g2_loaded", 16))
            pe.wait_ge(*ev.at("ck_y_out", NC))
            for h in range(HP):
                pe.wait_ge(*ev.at("y_final", h))
                column_sums(0, K("block_ones"), CUM[:, h, :]).then_inc(ev["y_sum"], 1)
                pe.wait_ge(*ev.at("y_sq", h + 1))
                column_sums(1, K("block_ones"), T[:, 1, :]).then_inc(ev["y_sq_sum"], 1)
                pe.wait_ge(*ev.at("bonus_prod", h + 1))
                column_sums(0, K("block_ones"), T[:, 1, :]).then_inc(ev["bonus_sum"], 1)
                column_sums(1, G2[:, h * P:(h + 1) * P], Z[:, 13, :]).then_inc(ev["g_made"], 1)
            pe.wait_ge(*ev.at("y_final", HP))

            pe.wait_ge(*ev.at("ya_split", HP))
            pe.wait_ge(*ev.at("yb_split", HP))

            def merge(i, end):
                for s in range(2):
                    pe.wait_ge(*ev.at(f"w_split{s}", i + (AT_MERGE + 1)))
                    pe.wait_ge(*ev.at(f"psum_free{s}", i + AT_MERGE))
                    pe.wait_ge(*ev.at(f"psum_free{1 - s}", i + (AT_MERGE + s)))
                    product(0, YA, HP, 0, s)
                    product(1, YB, HP, HP, s).then_inc(ev[f"unit_done{s}"], 1)
            loop(pe, KT // 2, merge)
            pe.wait_ge(*ev.at("merged", KT))
            pe.wait_ge(*ev.at("psum_free1", AT_OUT))
            units(AT_OUT, KT, M)
            norm(2)
            pe.wait_ge(*ev.at("h_ready", 3 * KT))
            ffn(AT_FFN2, True)
            norm(3)
            pe.wait_ge(*ev.at("h_full", 4 * KT))
            for t in range(9):
                n = P if t < 8 else NS
                if t >= 2:
                    pe.wait_ge(*ev.at(f"y_moved{t % 2}", t // 2))
                base = 1024 * (t % 2)
                for k in range(KT):
                    last = nc.tensor.transpose(PSf[0:n, base + k * P:base + (k + 1) * P], X[:, k, t * P:t * P + n], K("ident"))
                last.then_inc(ev["y_trans"], 1)


_INS = ["x_prompt", "x_sample", "cache_k", "cache_v", "state_wkv", "state_shift", "page_table",
        "ffn1_norm", "ffn1_up", "ffn1_down", "mix_norm", "w_in", "gate_bias",
        "rw_mu", "rw_w0", "rw_w2", "rw_a0", "rw_a2", "rw_g2", "rw_k_k", "rw_k_a", "rw_r_k", "rw_ln_w", "rw_ln_b",
        "da_lq1", "da_lk1", "da_lq2", "da_lk2", "da_subln", "w_proj_a", "w_proj_b", "w_out",
        "ffn2_norm", "ffn2_up", "ffn2_down", "final_norm"]
_OUTS = [("y_prompt", (1, NP, D)), ("y_sample", (NS, 1, D)),
         ("k_prompt", (1, 1, NP, 8, 64)), ("v_prompt", (1, 1, NP, 4, 128)),
         ("wkv_prompt", (1, 1, 8, 64, 64)), ("shift_prompt", (1, 1, RW_COLS)),
         ("k_sample", (1, NS, 1, 8, 64)), ("v_sample", (1, NS, 1, 4, 128)),
         ("wkv_sample", (1, NS, 8, 64, 64)), ("shift_sample", (1, NS, RW_COLS))]


def kernel(**inputs):
    import numpy as _np
    import concourse.bacc as _bacc
    from concourse import mybir as _mybir
    from concourse.bass_utils import run_bass_kernel_spmd as _run

    nc = _bacc.Bacc("TRN2", target_bir_lowering=False, num_devices=1)
    arrays, A = {}, {}
    for name in _INS:
        a = _np.ascontiguousarray(inputs[name])
        arrays["in_" + name] = a
        A[name] = nc.dram_tensor("in_" + name, a.shape, _mybir.dt.from_np(a.dtype), kind="ExternalInput").ap()
    for name, a in zip(("const_table", "const_rotary", "const_fresh"), shape_constants()):
        arrays[name] = _np.ascontiguousarray(a)
        A[name] = nc.dram_tensor(name, a.shape, F32, kind="ExternalInput").ap()
    for name, shape in _OUTS:
        A[name] = nc.dram_tensor("out_" + name, shape, F32, kind="ExternalOutput").ap()
    build(nc, A)
    r = _run(nc, [arrays], core_ids=[0])
    return tuple(r.results[0]["out_" + name] for name, _ in _OUTS)
```

```python
import concourse.bass as bass
from concourse import mybir
from concourse.alu_op_type import AluOpType as ALU
from contextlib import ExitStack
import math
import numpy as np

F32 = mybir.dt.float32
F32R = mybir.dt.float32r
I32 = mybir.dt.int32
ACT = mybir.ActivationFunctionType
AX = mybir.AxisListType.X
ds = bass.ds

P = 128
D = 1024
KT = D // P
NP = 1024
NS = 8
NT = NP + NS
NCH = 3
CH = NT // NCH
FT = 22
GROUP = 8
RW = 512
RW_COLS = 3 * RW + 256
ZT = RW_COLS // P
HP = 4
QT0, VT0, GT0 = ZT, ZT + 2 * HP, ZT + 3 * HP
GT = 2 * KT
C = 64
NC = NP // C
PAGES = 16
PAGE = 128
N_PHYS = 160
EPS = 1e-6
GN_EPS = 1e-5 * 64 * 64
LAM_INIT = 0.8 - 0.6 * math.exp(0.0)
SCALE = 64 ** -0.5
LOGDECAY = -math.exp(-0.5)
LEVELS = 5

PARAMS = [("ffn1_norm", 8), ("mix_norm", 8), ("ffn2_norm", 8), ("final_norm", 8), ("gate_bias", 16),
          ("rw_mu", ZT), ("rw_w0", 4), ("rw_a0", 4), ("rw_k_k", 4), ("rw_k_a", 4), ("rw_r_k", 4),
          ("rw_ln_w", 4), ("rw_ln_b", 4), ("da_subln", 4)]
ROW = {}
NROWS = 0
for _name, _n in PARAMS:
    ROW[_name] = NROWS
    NROWS += _n
ROW["lambda"] = NROWS
NROWS += 2

CONST_COLS = [("ident", 128), ("ones", 128), ("block_ones", 128), ("top_ones", 128), ("bottom_ones", 128),
              ("causal", 128), ("ident_stack", 64), ("strict_st", 64), ("incl_st", 64),
              ("pair_ts", 64), ("pair_st", 64)] + [(f"level{l}", 64) for l in range(LEVELS)]
CONST_AT = {}
NCONST = 0
for _name, _n in CONST_COLS:
    CONST_AT[_name] = NCONST
    NCONST += _n


def shape_constants():
    table = np.zeros((P, NCONST), np.float32)
    r = np.arange(P)

    def put(name, a):
        table[:, CONST_AT[name]:CONST_AT[name] + a.shape[1]] = a
    put("ident", np.eye(P))
    put("ones", np.ones((P, P)))
    put("block_ones", (r[:, None] // 64 == r[None, :] // 64) * 1.0)
    put("top_ones", (r[:, None] < 64) * np.ones((P, P)))
    put("bottom_ones", (r[:, None] >= 64) * np.ones((P, P)))
    put("causal", np.where(r[None, :] <= r[:, None], 0.0, -1e30))
    s, t = r[:, None] % 64, np.arange(64)[None, :]
    put("ident_stack", (s == t) * 1.0)
    put("strict_st", (s < t) * 1.0)
    put("incl_st", (s <= t) * 1.0)
    put("pair_ts", ((s // 2 == t // 2) & (s > t)) * 1.0)
    put("pair_st", ((s // 2 == t // 2) & (s < t)) * 1.0)
    for l in range(LEVELS):
        half = 2 << l
        put(f"level{l}", ((s // (2 * half) == t // (2 * half)) & (s // half % 2 == 0) & (t // half % 2 == 1)) * 1.0)
    pos = np.concatenate([np.arange(NP), np.full(NS, PAGES * PAGE)]).astype(np.float32)
    inv = (np.float32(10000.0) ** (-np.arange(32, dtype=np.float32) / np.float32(32))).astype(np.float32)
    ang = (pos[None, :] * inv[r % 32][:, None]).astype(np.float32)
    sign = np.where(r % 64 < 32, 1.0, -1.0).astype(np.float32)[:, None]
    rot = np.stack([np.cos(ang), np.sin(ang) * sign], 1).astype(np.float32)
    fresh = np.broadcast_to((np.arange(NP) % C != 0).astype(np.float32), (P, NP)).copy()
    return table, rot, fresh


LINES = [
    [("x_saved", 16), ("gate_saved0", 8 * GT)],
    [("rotary_loaded", 16), ("gate_saved1", 8 * GT)],
    [("x_moved1", 4), ("q_bc", NS), ("lam_exp", 1), ("k_tok_made", 9), ("s_exp", 2), ("probs_made", 64), ("o_sq", HP),
     ("z_act", 2), ("lora_act", 2 * HP), ("ck_p", 2 * NC), ("y_sq", HP), ("yb_high", HP), ("merge_high", KT), ("y_moved1", 4)],
    [("w_lo_moved", 32), ("o_root", HP), ("kk_sq", HP), ("ck_tok_moved", 4 * NC), ("y_root", HP)],
    [("o_moved", 32), ("w_sample", HP), ("ck_r_moved", NC), ("ya_high", HP)],
    [("kk_norm", HP), ("ck_t1_act", LEVELS * NC)],
    [("par_trans", 1), ("x_trans", KT), ("s_self", 1), ("q_rows", NS), ("lam_sums", 1), ("v_trans", 9), ("s_sum", 1),
     ("scores_done", 32), ("o_sq_sum", HP), ("z_rows_trans", 1), ("lora_made", HP), ("ck_gram", NC),
     ("wkv_trans", 1), ("rows_made", HP), ("y_sum", HP), ("y_trans", 9)],
    [("k_trans", 9), ("w_trans_lo", 32), ("kk_sum", HP), ("ck_tok", 4 * NC), ("y_sq_sum", HP)],
    [("w_trans_hi", 16), ("ck_r", NC), ("bonus_sum", HP)],
    [("o_done", 32), ("ck_t1", LEVELS * NC), ("g_made", HP)],
    [("par_moved", 2), ("x_moved0", 4), ("s_self_prod", 1), ("s_self_moved", 2), ("q_diag", NS), ("s_max_part", 1),
     ("v_tok_made", 9), ("s_shifted", 2), ("s_sum_part", 1), ("s_weights", 2), ("neg_max", 32), ("o_mean", HP), ("z_last", ZT), ("z_rows_made", 1),
     ("kk_scaled", HP), ("ck_zeroed", 1), ("ck_at", NC), ("wkv_made", 2), ("row_diag", 5 * HP),
     ("y_centred", HP), ("yb_split", HP), ("merge_full", KT), ("y_moved0", 5)],
    [("lam_prod", 1), ("yb_done", HP),
     ("ld_made", HP), ("ck_bt", NC), ("state_new", HP), ("y_var", HP)],
    [("ck_kt", 2 * NC),
     ("bonus_prod", HP), ("merged", KT)],
    [("ck_rt", NC)],
    [("pre_done", HP), ("y_final", HP)],
    [("ck_x", NC), ("ya_split", HP)],
    [("w_ready", 32), ("ck_ys", LEVELS * NC)],
    [("w_hi_moved", 16), ("ck_ar", NC)],
]


PRIMED = {
    "scalar": ["ck_y_out"],
    "vector": ["w_split0", "w_split1", "psum_free0", "psum_free1", "ff_full", "z_mixed0", "z_mixed1",
               "k_used0", "k_used1", "k_used2", "k_used3", "ck_state", "ck_s"],
    "tensor": ["unit_done0", "unit_done1", "ck_u"],
}


class Events(dict):
    def __init__(self, nc, ctx):
        super().__init__()
        self.nc, self.ctx, self.base = nc, ctx, {}
        for line in LINES:
            shared, total = self.make(line[0][0]), 0
            for name, n in line:
                self[name], self.base[name] = shared, total
                total += n
        for names in PRIMED.values():
            self.base.update((name, 1) for name in names)

    def prime(self, eng, engine):
        for name in PRIMED[engine]:
            eng.sem_inc(self[name], 1)

    def make(self, name):
        return self.ctx.enter_context(self.nc.semaphore("s_" + name))

    def __missing__(self, name):
        self[name] = self.make(name)
        return self[name]

    def at(self, name, n):
        return self[name], n + self.base.get(name, 0)


def build(nc, A):
    ctx = ExitStack()
    with ctx:
        ev = Events(nc, ctx)

        base = (nc.sbuf_base + 63) // 64 * 64
        TILE = NT * 4
        place = [base]

        def at(name, cols, offset=None, dt=F32):
            if offset is None:
                offset = place[0]
                place[0] = (place[0] + cols * 4 + 31) // 32 * 32
            return nc.alloc_sbuf_tensor_at(name, [P, cols], dt, offset=offset)

        stg = [at(f"w_stage{s}", KT * P)[:, :].rearrange("p (k n) -> p k n", n=P) for s in range(2)]
        whi = [at(f"w_hi{s}", KT * P, dt=F32R)[:, :].rearrange("p (k n) -> p k n", n=P) for s in range(2)]
        wlo = [at(f"w_lo{s}", KT * P, dt=F32R)[:, :].rearrange("p (k n) -> p k n", n=P) for s in range(2)]
        arena = place[0]
        place[0] += 40 * TILE

        def tiles(name, first, n, dt=F32):
            return at(name, n * NT, arena + first * TILE, dt)[:, :].rearrange("p (k n) -> p k n", n=NT)

        def cols(name, first, n):
            return at(name, n, arena + first * TILE)[:, :]

        T = at("tmp", 2 * NT)[:, :].rearrange("p (s n) -> p s n", n=NT)
        rstd = at("rstd", NT)[:, :]
        const = at("const", NCONST)[:, :]
        par = at("par", NROWS)[:, :]
        zlast = at("z_last", 9 * ZT)[:, :].rearrange("p (j m) -> p j m", m=ZT)
        zshift = at("z_shift", NS * ZT)[:, :].rearrange("p (b m) -> p b m", m=ZT)
        vsam = at("v_sample", HP * NS)[:, :].rearrange("p (h b) -> p h b", b=NS)
        small = at("small", 64)[:, :]
        idle = at("idle", 4)[:, :]
        wsam = at("decay_sample", HP * NS)[:, :].rearrange("p (h b) -> p h b", b=NS)
        ptab = nc.alloc_sbuf_tensor_at("pages", [1, NS * PAGES], I32, offset=place[0])
        place[0] += NS * PAGES * 4
        assert place[0] <= nc.sbuf_usable_end, (place[0], nc.sbuf_usable_end)

        def K(name, n=None):
            width = n or dict(CONST_COLS)[name]
            return const[:, CONST_AT[name]:CONST_AT[name] + width]

        def param(name, i=0, n=1):
            return par[:, ROW[name] + i:ROW[name] + i + n]

        X = tiles("x_res", 0, KT)
        H = [tiles("h_hi", 8, KT, F32R), tiles("h_lo", 16, KT, F32R)]
        G = [tiles("ff_hi", 24, GROUP, F32R), tiles("ff_lo", 32, GROUP, F32R)]
        xin = cols("x_in", 24, 9 * D).rearrange("p (t n) -> p t n", n=D)
        prow = cols("param_rows", 38, P)
        srow = cols("shift_rows", 39, P)
        Q = tiles("q_rot", 0, HP)
        Kr = tiles("k_rot", 4, HP)
        Vt = tiles("v_feat", 24, HP)
        rot = tiles("rotary", 28, 2)
        Vtok = cols("v_tok", 30, 8 * 512).rearrange("p (t n) -> p t n", n=512)
        pr = tiles("probs", 34, 4)[:, :, 0:NP].rearrange("p (s m) n -> p s m n", m=2)
        wT = [cols(f"w_trans{s}", 38 + s, NP) for s in range(2)]
        kout = [cols(f"k_out{s}", 34 + s, 512) for s in range(2)]
        kring = cols("key_ring", 30, 16 * 512).rearrange("p (g j n) -> p g j n", g=4, j=4)
        vring = cols("value_ring", 24, 8 * 512).rearrange("p (g j n) -> p g j n", g=2, j=4)
        prod = cols("kq_prod", 38, 4 * 512)
        SC = cols("score_sums", 28, 1024)
        Qbc = cols("q_bcast", 29, 512)
        Wp = cols("s_weights", 29, 512)
        Qdg = tiles("q_diag", 29, 1)[:, 0, 512:1024]
        sm = rstd[:, 0:512]
        osum = rstd[:, 512:1024]
        smax, sself, ssum, sexp = sm[:, 0:64], sm[:, 64:128], sm[:, 128:192], sm[:, 192:256]
        wself, qk_cols = sm[:, 256:288], sm[:, 320:352]
        smaxp, vw = sm[:, 352:416], sm[:, 416:420]
        Z = tiles("z_mix", 24, ZT)
        Rf, Kf, Vf = Z[:, 0:4], Z[:, 4:8], Z[:, 8:12]
        CUM = tiles("cum_y", 4, HP)
        KKn = tiles("kk", 16, HP)
        Bf = tiles("b_vec", 20, HP)
        lw2 = cols("lora_w2a2", 38, 512)
        lg2 = cols("lora_g2", 39, 512)
        fresh = cols("fresh", 15, NP)
        pools = [[at("chunk_work", 8 * NT, arena + 8 * TILE)[:, :], 0],
                 [at("chunk_work2", 2 * NT, arena + 38 * TILE)[:, :], 0],
                 [at("chunk_work3", 4 * KT * P, base + 2 * KT * P * 4)[:, :], 0],
                 [T.rearrange("p s n -> p (s n)"), 0], [Z[:, 12, :], 0], [rstd, 0]]

        def work(n):
            for p in pools:
                if p[1] + n <= p[0].shape[1]:
                    p[1] += n
                    return p[0][:, p[1] - n:p[1]]
            assert False, "the chunk loop's buffers are full"

        def heads(n, count=2):
            return [work(HP * n).rearrange("p (h n) -> p h n", h=HP) for _ in range(count)]
        atd, btd, ktd, vtd, aakd, btmd, Yd, Sd = [heads(P) for _ in range(8)]
        Ud = heads(P, 1)[0]
        T1d = vtd
        zeroed = atd + btd + ktd + vtd + aakd + btmd + Yd + Sd + [Ud]
        ar = [a.rearrange("p h (a t) -> p h a t", a=2) for a in heads(P)]
        btok, ktok, vtok = [heads(P) for _ in range(3)]
        Pb = heads(65)
        bts, vts, Ys, LTs, arbs, arks, Xs, T1s = [heads(64) for _ in range(8)]
        Pinv = T1s
        Rs, Us, Ss = heads(64, 3)
        St = at("state", 2 * KT * P, base)[:, :].rearrange("p (h b j) -> p h b j", h=HP, b=NS)
        dg = cols("row_diag", 10, 5 * 512).rearrange("p (v b j) -> p v b j", v=5, b=NS)
        stm = cols("state_tmp", 13, 512).rearrange("p (b j) -> p b j", b=NS)
        sa = small[:, 8:16]
        wfin = cols("wkv_out", 14, HP * 64).rearrange("p (h n) -> p h n", h=HP)
        zrow = cols("z_rows", 14, P)
        G2 = cols("lora_g2b", 15, 512)
        YA = [tiles("ya_hi", 16, HP, F32R), tiles("ya_lo", 20, HP, F32R)]
        YB = [tiles("yb_hi", 8, HP, F32R), tiles("yb_lo", 12, HP, F32R)]
        M = [tiles("merged_hi", 32, KT, F32R), tiles("merged_lo", 24, KT, F32R)]
        gring = tiles("gate_ring", 4, 4).rearrange("p (s a) n -> p s a n", a=2)
        yout = [cols(f"y_out{s}", 24 + s, D) for s in range(2)]

        x_save = nc.dram_tensor("x_save", (KT, P, NT), F32).ap()
        g_save = nc.dram_tensor("gate_save", (GT, P, NT), F32).ap()

        PS = ctx.enter_context(nc.psum_tensor("ps", [P, 8, 512], F32))
        PSf = PS[:, :, :].rearrange("p a n -> p (a n)")
        dense = [PS[:, 3 * s:3 * s + 3, 0:CH] for s in range(2)]

        def ch3(a):
            return a.rearrange("p (c n) -> p c n", c=NCH)

        def ps4(bank, first=0, n=64):
            return PS[:, bank, first:first + HP * n].rearrange("p (h n) -> p h n", h=HP)

        def rows(name):
            return A[name].rearrange("(r n) -> r n", n=P) if len(A[name].shape) == 1 else \
                A[name].rearrange("l (r n) -> (l r) n", n=P)

        w_in = A["w_in"][0]
        wsrc = {n: A[n][0].rearrange("(k p) n -> p k n", p=P)
                for n in ("ffn1_up", "ffn1_down", "ffn2_up", "ffn2_down", "w_in", "w_proj_a", "w_proj_b", "w_out")}
        ck = A["cache_k"].rearrange("l n t m d -> (l n) t (m d)")
        cv = A["cache_v"].rearrange("l n t h d -> (l n) t (h d)")

        GROUPS = [(0, 8), (8, 8), (16, 6)]
        PAIRS_FFN = FT + len(GROUPS) * KT // 2
        AT_QK = PAIRS_FFN
        AT_V = AT_QK + HP
        AT_GATES = AT_V + HP // 2
        AT_Z = AT_GATES + GT // 2
        AT_MERGE = AT_Z + ZT // 2
        AT_OUT = AT_MERGE + KT // 2
        AT_FFN2 = AT_OUT + KT // 2

        def loop(eng, n, body, end=False):
            if n - end > 0:
                with eng.Fori(0, n - end) as i:
                    body(i, False)
            if end:
                body(n - 1, True)

        def flat(a):
            return a.rearrange("p a n -> p (a n)")

        def bc(a, n):
            return a.broadcast_to([a.shape[0], a.shape[1], n])

        def over_heads(a):
            return a.unsqueeze(1).broadcast_to([a.shape[0], HP, a.shape[1]])

        halves = (slice(0, 64), slice(64, 128))

        def settle(eng):
            if eng is nc.scalar:
                nc.scalar.activation(idle[:, 0:1], idle[:, 1:2], ACT.Copy)
            else:
                nc.gpsimd.tensor_tensor(idle[:, 2:3], idle[:, 1:2], idle[:, 1:2], ALU.add)
            eng.drain()

        STEPS = 8 * HP
        FILL_STEP = [s for s in range(HP, STEPS) for _ in range(2 if s >= STEPS - HP else 1)]

        def level(i, l, x):
            return i * (2 * LEVELS) + (2 * l + x + 1)

        AB_PS, AK_PS = [ps4(0, 0, 128), ps4(4, 0, 128)], [ps4(1, 0, 128), ps4(5, 0, 128)]
        T1_PS = [ps4(2), ps4(6)]
        D_PS = [PS[:, b, :].rearrange("p (h n) -> p h n", n=64) for b in (1, 5)]
        R_PS, U_PS, DS_PS, Y_PS = ps4(2), ps4(6), ps4(3), ps4(7)
        TOKEN_MAJOR = [(vts[0], ps4(3)), (vtok[0], ps4(7, 0, 128)), (vts[1], ps4(3)), (vtok[1], ps4(7, 0, 128)),
                       (btok[0], ps4(3, 0, 128)), (btok[1], ps4(7, 0, 128)),
                       (ktok[0], ps4(3, 0, 128)), (ktok[1], ps4(7, 0, 128))]

        VIEW_SC = SC.rearrange("p (b g m) -> p b g m", b=NS, g=PAGES)
        VIEW_W = Wp.rearrange("p (b g h) -> p b g h", b=NS, g=PAGES)

        block = ctx.enter_context(nc.Block())

        @block.sync
        def _(sp):
            def load_unit(s, c, src, nk=KT, second=None):
                sp.wait_ge(*ev.at(f"w_split{s}", c))
                h = HP
                sp.dma_start(stg[s][:, 0:h, :], src[:, 0:h]).then_inc(ev[f"w_loaded{s}"], 16)
                sp.dma_start(stg[s][:, h:nk, :], src[:, h:nk] if second is None else second)\
                    .then_inc(ev[f"w_loaded{s}"], 16)

            sp.dma_start(const, A["const_table"]).then_inc(ev["params_loaded"], 16)
            for name, n in PARAMS:
                src = A[name].rearrange("l h n -> l (h n)") if name == "rw_r_k" else A[name]
                src = src.rearrange("(r n) -> r n", n=P) if len(src.shape) == 1 else \
                    src.rearrange("l (r n) -> (l r) n", n=P)
                sp.dma_start(prow[ROW[name]:ROW[name] + n, :], src).then_inc(ev["params_loaded"], 16)
            for i, name in enumerate(("da_lq1", "da_lq2", "da_lk1", "da_lk2")):
                r = ROW["lambda"] + i // 2
                sp.dma_start(prow[r:r + 1, (i % 2) * 64:(i % 2) * 64 + 64], A[name])\
                    .then_inc(ev["params_loaded"], 16)
            sp.dma_start(srow[0:NS * ZT, :], A["state_shift"][0].rearrange("b (m p) -> (b m) p", p=P))\
                .then_inc(ev["params_loaded"], 16)
            sp.dma_start(ptab[:, :], A["page_table"].rearrange("(a b) n -> a (b n)", a=1))\
                .then_inc(ev["pages_loaded"], 16)
            for t in range(8):
                sp.dma_start(xin[:, t, :], A["x_prompt"][0, t * P:(t + 1) * P, :]).then_inc(ev["x_loaded"], 16)
            sp.dma_start(xin[0:NS, 8, :], A["x_sample"][:, 0, :]).then_inc(ev["x_loaded"], 16)

            def ffn_loads(first, up, down):
                for j0, n in GROUPS:
                    with sp.Fori(0, n) as i:
                        for s in range(2):
                            load_unit(s, i + first, wsrc[up][:, :, ds((i + (j0 + s * FT)) * P, P)])
                    first += n
                    with sp.Fori(0, KT // 2) as i:
                        for s in range(2):
                            load_unit(s, i + first, wsrc[down][:, j0:j0 + n, ds((i * 2 + s) * P, P)], n)
                    first += KT // 2

            def w_loads(first, name, tile, n):
                with sp.Fori(0, n // 2) as i:
                    for s in range(2):
                        load_unit(s, i + first, wsrc[name][:, :, ds((i * 2 + (tile + s)) * P, P)])

            ffn_loads(0, "ffn1_up", "ffn1_down")
            w_loads(AT_QK, "w_in", QT0, 3 * HP)

            def cache_page(slot, cache, at, done):
                page = sp.value_load(ptab[0:1, at], min_val=0, max_val=N_PHYS - 1)
                sp.dma_start(slot, cache[ds(page, 1)].rearrange("a t n -> (a t) n")).then_inc(ev[done], 16)

            sp.wait_ge(*ev.at("pages_loaded", 16))
            with sp.Fori(0, GT // 2) as i:
                for s in range(2):
                    load_unit(s, i + AT_GATES, wsrc["w_in"][:, :, ds((i * 2 + (GT0 + s)) * P, P)])
                    for g in (2 * s, 2 * s + 1):
                        sp.wait_ge(*ev.at(f"k_used{g}", i))
                        for j in range(4):
                            cache_page(kring[:, g, j, :], ck, ds(i * PAGES + (4 * g + j), 1), f"key_pages{g}")
            sp.wait_ge(*ev.at("v_trans", 9))
            sp.wait_ge(*ev.at("s_self_prod", 1))
            for f in range(4 * NS):
                if f >= 2:
                    sp.wait_ge(*ev.at("value_used", f - 1))
                for j in range(4):
                    cache_page(vring[:, f % 2, j, :], cv, slice(4 * f + j, 4 * f + j + 1), f"value_pages{f % 2}")
            w_loads(AT_Z, "w_in", 0, ZT)
            sp.wait_ge(*ev.at("unit_done1", AT_MERGE))
            sp.dma_start(lw2[0:64, :], A["rw_w2"][0]).then_inc(ev["lora_loaded"], 16)
            sp.dma_start(lw2[64:128, :], A["rw_a2"][0]).then_inc(ev["lora_loaded"], 16)
            sp.dma_start(fresh, A["const_fresh"]).then_inc(ev["lora_loaded"], 16)
            sp.wait_ge(*ev.at("w_split0", AT_MERGE))
            sp.wait_ge(*ev.at("w_split1", AT_MERGE))
            for b in range(NS):
                sp.dma_start(St[:, :, b, :], A["state_wkv"][0, b].rearrange("(h two) i j -> (two i) h j", two=2))\
                    .then_inc(ev["state_loaded"], 16)
            sp.wait_ge(*ev.at("wkv_trans", 1))
            sp.dma_start(G2, A["rw_g2"][0]).then_inc(ev["g2_loaded"], 16)
            sp.wait_ge(*ev.at("state_stored", 16 * NS))
            with sp.Fori(0, KT // 2) as i:
                for s in range(2):
                    load_unit(s, i + AT_MERGE, wsrc["w_proj_a"][:, :, ds((i * 2 + s) * P, P)],
                              second=wsrc["w_proj_b"][:, :, ds((i * 2 + s) * P, P)])
            w_loads(AT_OUT, "w_out", 0, KT)
            ffn_loads(AT_FFN2, "ffn2_up", "ffn2_down")

        @block.gpsimd
        def _(pool):
            pool.wait_ge(*ev.at("h_ready", 2 * KT))
            pool.dma_start(x_save.rearrange("k p n -> p k n"), X).then_inc(ev["x_saved"], 16)
            pool.dma_start(rot, A["const_rotary"]).then_inc(ev["rotary_loaded"], 16)
            with pool.Fori(0, GT // 2) as i:
                for s in range(2):
                    pool.wait_ge(*ev.at(f"psum_free{s}", i + (AT_GATES + 1)))
                    pool.dma_start(g_save[ds(i * 2 + s, 1)].rearrange("a p n -> (a p) n"), T[:, s, :])\
                        .then_inc(ev[f"gate_saved{s}"], 16)
            for t in range(9):
                n = P if t < 8 else NS
                pool.wait_ge(*ev.at("v_tok_made", t + 1))
                src = Vtok[:, t, :] if t < 8 else wT[1][:, 0:512]
                dst = A["v_prompt"][0, 0, t * P:(t + 1) * P].rearrange("t h d -> t (h d)") if t < 8 else \
                    A["v_sample"][0, :, 0].rearrange("t h d -> t (h d)")
                pool.dma_start(dst, src[0:n, :]).then_inc(ev["v_stored"], 16)
                pool.wait_ge(*ev.at("k_tok_made", t + 1))
                dst = A["k_prompt"][0, 0, t * P:(t + 1) * P].rearrange("t m d -> t (m d)") if t < 8 else \
                    A["k_sample"][0, :, 0].rearrange("t m d -> t (m d)")
                pool.dma_start(dst, kout[t % 2][0:n, :]).then_inc(ev[f"k_stored{t % 2}"], 16)
            pool.wait_ge(*ev.at("s_max_part", 1))
            nc.gpsimd.partition_all_reduce(smax, smaxp, P, bass.bass_isa.ReduceOp.max).then_inc(ev["s_max_all"], 1)
            pool.wait_ge(*ev.at("z_rows_made", 1))
            pool.dma_start(A["shift_prompt"][0].rearrange("b (m p) -> (b m) p", p=P), zrow[0:ZT, :])\
                .then_inc(ev["z_stored"], 16)
            pool.dma_start(A["shift_sample"][0].rearrange("b (m p) -> (b m) p", p=P), zrow[ZT:9 * ZT, :])\
                .then_inc(ev["z_stored"], 16)
            pool.wait_ge(*ev.at("ck_zeroed", 1))
            with pool.Fori(0, NC // 2) as i:
                pool.wait_ge(*ev.at("ck_u", i * 2))
                settle(nc.gpsimd)
                for x in range(2):
                    for q in halves:
                        nc.gpsimd.tensor_copy(vtd[x][q, :, q], Vf[q, :, ds(i * (2 * C) + x * C, C)])\
                            .then_inc(ev["ck_vtd"], 1)
                for l in range(LEVELS):
                    for x in range(2):
                        if l == 0:
                            pool.wait_ge(*ev.at("ck_lt", i * 2 + (x + 1)))
                        else:
                            pool.wait_ge(*ev.at("ck_t1", level(i, l - 1, x)))
                        for q in halves:
                            nc.gpsimd.tensor_tensor(btmd[x][q, :, q], LTs[x][q], over_heads(K(f"level{l}"))[q], ALU.mult)\
                                .then_inc(ev["ck_mask"], 1)
            pool.wait_ge(*ev.at("wkv_made", 2))
            for two in range(2):
                pool.dma_start(A["wkv_prompt"][0, 0].rearrange("(h two) i j -> two i h j", two=2)[two],
                               wfin[halves[two]]).then_inc(ev["wkv_stored"], 16)
            pool.wait_ge(*ev.at("state_new", HP))
            for b in range(NS):
                pool.dma_start(A["wkv_sample"][0, b].rearrange("(h two) i j -> (two i) h j", two=2), St[:, :, b, :])\
                    .then_inc(ev["state_stored"], 16)
            pool.wait_ge(*ev.at("ya_split", HP))
            pool.wait_ge(*ev.at("gate_saved0", 16 * (GT // 2)))
            pool.wait_ge(*ev.at("gate_saved1", 16 * (GT // 2)))
            with pool.Fori(0, KT // 2) as i:
                for s in range(2):
                    pool.wait_ge(*ev.at(f"psum_free{s}", i + AT_MERGE))
                    for a in range(2):
                        pool.dma_start(gring[:, s, a, :],
                                       g_save[ds(i * 2 + (s + a * KT), 1)].rearrange("a p n -> (a p) n"))\
                            .then_inc(ev[f"gates_back{s}"], 16)
            pool.wait_ge(*ev.at("merged", KT))
            pool.wait_ge(*ev.at("x_saved", 16))
            pool.dma_start(X, x_save.rearrange("k p n -> p k n")).then_inc(ev["x_back"], 16)
            for t in range(9):
                pool.wait_ge(*ev.at(f"y_moved{t % 2}", t // 2 + 1))
                dst = A["y_prompt"][0, t * P:(t + 1) * P, :] if t < 8 else A["y_sample"][:, 0, :]
                pool.dma_start(dst, yout[t % 2][0:P if t < 8 else NS, :]).then_inc(ev[f"y_stored{t % 2}"], 16)
            for name, n in (("y_stored0", 5), ("y_stored1", 4), ("v_stored", 9), ("k_stored0", 5), ("k_stored1", 4),
                            ("z_stored", 2), ("wkv_stored", 2), ("state_stored", NS)):
                pool.wait_ge(*ev.at(name, 16 * n))

        @block.scalar
        def _(act):
            ev.prime(act, "scalar")
            sc = nc.scalar

            def split(s, c):
                act.wait_ge(*ev.at(f"w_loaded{s}", (c + 1) * 32))
                act.wait_ge(*ev.at(f"unit_done{s}", c))
                sc.activation(whi[s], stg[s], ACT.Copy).then_inc(ev[f"w_high{s}"], 1)

            for k in range(1, KT, 2):
                act.wait_ge(*ev.at("x_trans", k + 1))
                sc.activation(X[:, k, :], PSf[:, 1536:1536 + NT], ACT.Copy).then_inc(ev["x_moved1"], 1)

            def norm(n, high=True):
                for k in range(KT):
                    if k == 0:
                        act.wait_ge(*ev.at("x_done", n + 1))
                    if k >= 2:
                        act.wait_ge(*ev.at("sq_used", n * KT + k - 1))
                    sc.activation(T[:, k % 2, :], X[:, k, :], ACT.Square).then_inc(ev["sq_made"], 1)
                act.wait_ge(*ev.at("mean_made", n + 1))
                sc.activation(rstd, rstd, ACT.Sqrt).then_inc(ev["root_made"], 1)
                if high:
                    for k in range(KT):
                        act.wait_ge(*ev.at("h_full", n * KT + k + 1))
                        sc.activation(H[0][:, k, :], T[:, k % 2, :], ACT.Copy).then_inc(ev["h_high"], 1)

            def ffn(first, pairs, last):
                for gi, (j0, n) in enumerate(GROUPS):
                    def up(i, end):
                        c = i + first
                        split(1, c)
                        act.wait_ge(*ev.at("unit_done0", c + 1))
                        act.wait_ge(*ev.at("ff_full", i + pairs))
                        sc.activation(ch3(T[:, 0, :]), dense[0], ACT.Silu).then_inc(ev["psum_free0"], 1)
                        split(0, c + 1)
                        act.wait_ge(*ev.at("ff_full", i + (pairs + 1)))
                        settle(nc.scalar)
                        sc.activation(flat(G[0][:, ds(i, 1), :]), T[:, 1, :], ACT.Copy).then_inc(ev["ff_high"], 1)
                    loop(act, n, up)
                    first += n
                    pairs += n

                    def down(i, end):
                        split(1, i + first)
                        if not end:
                            split(0, i + (first + 1))
                    loop(act, KT // 2, down, last and gi == len(GROUPS) - 1)
                    first += KT // 2

            split(0, 0)
            norm(0)
            ffn(0, 0, False)
            norm(1)

            def qk(i, end):
                split(1, i + AT_QK)
                split(0, i + (AT_QK + 1))
            loop(act, HP, qk)

            def values(i, end):
                for s in range(2):
                    split(1 - s, i + (AT_V + s))
                    act.wait_ge(*ev.at(f"unit_done{s}", i + (AT_V + 1)))
                    settle(nc.scalar)
                    sc.activation(flat(Vt[:, ds(i * 2 + s, 1), :]).rearrange("p (c n) -> p c n", c=NCH), dense[s],
                                  ACT.Copy).then_inc(ev[f"psum_free{s}"], 1)
            loop(act, HP // 2, values)

            def gates(i, end):
                for s in range(2):
                    if s == 0 or not end:
                        split(1 - s, i + (AT_GATES + s))
                    act.wait_ge(*ev.at(f"unit_done{s}", i + (AT_GATES + 1)))
                    act.wait_ge(*ev.at(f"gate_saved{s}", 16 * i))
                    settle(nc.scalar)
                    sc.activation(ch3(T[:, s, :]), dense[s], ACT.Sigmoid,
                                  bias=par[:, ds(i * 2 + (ROW["gate_bias"] + s), 1)]).then_inc(ev[f"psum_free{s}"], 1)
                    if s == 0:
                        act.wait_ge(*ev.at("q_rows", i + 1))
                        act.wait_ge(*ev.at("k_used3", i))
                        sc.activation(Qbc, PS[:, 6, :], ACT.Copy).then_inc(ev["q_bc"], 1)
            act.wait_ge(*ev.at("rope_done", 2 * HP))
            loop(act, GT // 2, gates, True)

            act.wait_ge(*ev.at("lam_sums", 1))
            sc.activation(small[:, 0:2], PS[:, 7, 0:2], ACT.Exp).then_inc(ev["lam_exp"], 1)
            act.wait_ge(*ev.at("k_used3", NS))
            for t in range(9):
                n = P if t < 8 else NS
                act.wait_ge(*ev.at("k_trans", t + 1))
                if t >= 2:
                    act.wait_ge(*ev.at(f"k_stored{t % 2}", 16 * (t // 2)))
                sc.activation(kout[t % 2][0:n, :], PS[0:n, 2 + t % 2, :], ACT.Copy).then_inc(ev["k_tok_made"], 1)
            act.wait_ge(*ev.at("k_stored0", 16 * 5))
            act.wait_ge(*ev.at("k_stored1", 16 * 4))
            act.wait_ge(*ev.at("v_stored", 16 * 9))

            act.wait_ge(*ev.at("s_shifted", 2))
            sc.activation(SC, SC, ACT.Exp, scale=SCALE).then_inc(ev["s_exp"], 1)
            sc.activation(sexp, sself, ACT.Exp, scale=SCALE).then_inc(ev["s_exp"], 1)

            def probs(step):
                s, n = step % 2, (step // HP + 1) * P
                act.wait_ge(*ev.at("neg_max", step + 1))
                if step >= 2:
                    act.wait_ge(*ev.at("o_done", step - 1))
                for m in range(2):
                    sc.activation(pr[:, s, m, 0:n], PSf[:, m * 1024:m * 1024 + n], ACT.Exp,
                                  bias=small[:, 16 + 4 * s + m:17 + 4 * s + m], scale=SCALE,
                                  accum_out=small[:, 18 + 4 * s + m:19 + 4 * s + m]).then_inc(ev["probs_made"], 1)
            probs(0)
            for step in range(STEPS):
                qi, s = step // HP, step % 2
                act.wait_ge(*ev.at("w_trans_lo", step + 1))
                lo = min(4, qi + 1) * P
                sc.activation(wT[s][:, 0:lo], PS[:, 4, 0:lo], ACT.Copy).then_inc(ev["w_lo_moved"], 1)
                if step + 1 < STEPS:
                    probs(step + 1)
                act.wait_ge(*ev.at("o_done", step + 1))
                sc.activation(Q[:, step % HP, qi * P:(qi + 1) * P], PS[:, 6, 0:P], ACT.Copy)\
                    .then_inc(ev["o_moved"], 1)
                for b in range(NS):
                    if FILL_STEP[4 * b + 3] == step:
                        act.wait_ge(*ev.at("value_used", 4 * b + 4))
                        sc.activation(osum[0:HP, :], PS[0:HP, 7, :], ACT.Copy).then_inc(ev["osum_moved"], 1)

            for h in range(HP):
                act.wait_ge(*ev.at("o_sample", NS))
                if h >= 2:
                    act.wait_ge(*ev.at("o_mean", h - 1))
                sc.activation(T[:, h % 2, :], Q[:, h, :], ACT.Square).then_inc(ev["o_sq"], 1)
                act.wait_ge(*ev.at("o_mean", h + 1))
                sc.activation(rstd, rstd, ACT.Sqrt).then_inc(ev["o_root"], 1)

            act.wait_ge(*ev.at("yb_done", HP))
            split(0, AT_Z)

            def z_raw(i, end):
                for s in range(2):
                    if s == 0 or not end:
                        split(1 - s, i + (AT_Z + s))
                    act.wait_ge(*ev.at(f"unit_done{s}", i + (AT_Z + 1)))
                    act.wait_ge(*ev.at(f"z_mixed{s}", i))
                    sc.activation(ch3(T[:, s, :]), dense[s], ACT.Copy).then_inc(ev[f"psum_free{s}"], 1)
            loop(act, ZT // 2, z_raw, True)

            act.wait_ge(*ev.at("z_mixed0", ZT // 2))
            act.wait_ge(*ev.at("z_mixed1", ZT // 2))
            sc.activation(Z[0:64, 12, :], Z[0:64, 12, :], ACT.Tanh).then_inc(ev["z_act"], 1)
            sc.activation(Z[:, 13, :], Z[:, 13, :], ACT.Sigmoid).then_inc(ev["z_act"], 1)
            for h in range(HP):
                act.wait_ge(*ev.at("lora_made", h + 1))
                act.wait_ge(*ev.at("pre_done", h))
                sc.activation(ch3(T[:, 0, :]), dense[0], ACT.Sigmoid, bias=param("rw_w0", h)).then_inc(ev["lora_act"], 1)
                sc.activation(ch3(Bf[:, h, :]), dense[1], ACT.Sigmoid, bias=param("rw_a0", h)).then_inc(ev["lora_act"], 1)
                act.wait_ge(*ev.at("kk_scaled", h + 1))
                sc.activation(T[:, 1, :], KKn[:, h, :], ACT.Square).then_inc(ev["kk_sq"], 1)
                act.wait_ge(*ev.at("ld_made", h + 1))
                sc.activation(wsam[:, h, :], T[:, 0, NP:NT], ACT.Exp).then_inc(ev["w_sample"], 1)
                act.wait_ge(*ev.at("kk_sum", h + 1))
                sc.activation(ch3(T[:, 1, :]), dense[0], ACT.Sqrt).then_inc(ev["kk_norm"], 1)

            act.wait_ge(*ev.at("pre_done", HP))
            act.wait_ge(*ev.at("ck_zeroed", 1))
            with act.Fori(0, NC // 2) as i:
                act.wait_ge(*ev.at("ck_state", i * 2))
                settle(nc.scalar)
                for x in range(2):
                    now = ds(i * (2 * C) + x * C, C)
                    sc.activation(Pb[x][:, :, 1:65], CUM[:, :, now], ACT.Exp).then_inc(ev["ck_p"], 1)
                    sc.activation(Pinv[x], CUM[:, :, now], ACT.Exp, scale=-1.0).then_inc(ev["ck_p"], 1)
                lo, hi = halves
                for x in range(2):
                    act.wait_ge(*ev.at("ck_bt", i * 2 + (x + 1)))
                    sc.activation(btd[x][lo, :, lo], bts[x][lo], ACT.Copy)
                    sc.activation(btd[x][hi, :, hi], bts[x][hi], ACT.Copy).then_inc(ev["ck_btd"], 1)
                    act.wait_ge(*ev.at("ck_at", i * 2 + (x + 1)))
                    sc.activation(atd[x][lo, :, lo], ar[x][lo, :, 0, :], ACT.Copy)
                    sc.activation(atd[x][hi, :, hi], ar[x][hi, :, 0, :], ACT.Copy).then_inc(ev["ck_atd"], 1)

                def move(k):
                    act.wait_ge(*ev.at("ck_tok", i * 8 + (k + 1)))
                    dst, src = TOKEN_MAJOR[k]
                    sc.activation(dst, src, ACT.Copy).then_inc(ev["ck_tok_moved"], 1)
                for k in range(4):
                    move(k)
                for l in range(LEVELS):
                    for x in range(2):
                        act.wait_ge(*ev.at("ck_t1", level(i, l, x)))
                        if l < LEVELS - 1:
                            sc.activation(T1s[x][hi], T1_PS[x][hi], ACT.Copy)
                        sc.activation(T1d[x][hi, :, hi], T1_PS[x][hi], ACT.Copy).then_inc(ev["ck_t1_act"], 1)
                    if l < 2:
                        move(4 + 2 * l)
                        move(5 + 2 * l)
                    for x in range(2):
                        act.wait_ge(*ev.at("ck_ys", level(i, l, x)))
                        sc.activation(Yd[x][hi, :, hi], Ys[x][hi], ACT.Copy).then_inc(ev["ck_yd_act"], 1)
                for x in range(2):
                    act.wait_ge(*ev.at("ck_r", i * 2 + (x + 1)))
                    sc.activation(Rs, R_PS, ACT.Copy).then_inc(ev["ck_r_moved"], 1)
                    act.wait_ge(*ev.at("ck_u", i * 2 + (x + 1)))
                    sc.activation(Us[hi], U_PS[hi], ACT.Copy)
                    sc.activation(Ud[hi, :, hi], U_PS[hi], ACT.Copy).then_inc(ev["ck_u_act"], 1)
                    act.wait_ge(*ev.at("ck_y", i * 2 + (x + 1)))
                    settle(nc.scalar)
                    sc.activation(CUM[:, :, ds(i * (2 * C) + x * C, C)], Y_PS, ACT.Copy).then_inc(ev["ck_y_out"], 1)

            for h in range(HP):
                act.wait_ge(*ev.at("y_centred", h + 1))
                sc.activation(T[:, 1, :], T[:, 0, :], ACT.Square).then_inc(ev["y_sq"], 1)
                act.wait_ge(*ev.at("y_var", h + 1))
                sc.activation(rstd, rstd, ACT.Sqrt).then_inc(ev["y_root"], 1)
                act.wait_ge(*ev.at("y_final", h + 1))
                sc.activation(YA[0][:, h, :], T[:, 0, :], ACT.Copy).then_inc(ev["ya_high"], 1)
            act.wait_ge(*ev.at("ya_split", HP))
            act.wait_ge(*ev.at("wkv_stored", 32))
            for h in range(HP):
                sc.activation(YB[0][:, h, :], Q[:, h, :], ACT.Copy).then_inc(ev["yb_high"], 1)

            split(0, AT_MERGE)

            def merge(i, end):
                for s in range(2):
                    split(1 - s, i + (AT_MERGE + s))
                    act.wait_ge(*ev.at("merge_full", i * 2 + (s + 1)))
                    settle(nc.scalar)
                    sc.activation(flat(M[0][:, ds(i * 2 + s, 1), :]), T[:, 0, :], ACT.Copy).then_inc(ev["merge_high"], 1)
            loop(act, KT // 2, merge)

            def out(i, end):
                split(1, i + AT_OUT)
                split(0, i + (AT_OUT + 1))
            loop(act, KT // 2, out)
            norm(2)
            ffn(AT_FFN2, FT, True)
            norm(3, False)
            for t in range(1, 9, 2):
                act.wait_ge(*ev.at("y_trans", t + 1))
                if t >= 3:
                    act.wait_ge(*ev.at("y_stored1", 16 * (t // 2)))
                sc.activation(yout[1], PSf[:, 1024:2048], ACT.Copy).then_inc(ev["y_moved1"], 1)

        @block.vector
        def _(dve):
            ev.prime(dve, "vector")
            v = nc.vector

            def in_turn(instruction):
                dve.drain()

            def split(s, c):
                dve.wait_ge(*ev.at(f"w_high{s}", c + 1))
                in_turn(v.tensor_tensor(wlo[s], stg[s], whi[s].bitcast(F32), ALU.subtract).then_inc(ev[f"w_split{s}"], 1))

            in_turn(v.memset(idle, 0.0))
            dve.wait_ge(*ev.at("par_trans", 1))
            in_turn(v.tensor_copy(par, PS[:, 7, 0:NROWS]).then_inc(ev["par_moved"], 1))
            in_turn(v.tensor_copy(zshift, PS[:, 7, P:P + NS * ZT].rearrange("p (b m) -> p b m", m=ZT)).then_inc(ev["par_moved"], 1))
            dve.wait_ge(*ev.at("par_moved", 2))
            in_turn(v.tensor_scalar(param("da_subln", 0, HP), param("da_subln", 0, HP), 1.0 - LAM_INIT, None, ALU.mult))
            in_turn(v.tensor_scalar(small[:, 32:36], param("rw_k_a", 0, HP), -1.0, 1.0, ALU.mult, ALU.add))
            in_turn(v.tensor_tensor(small[:, 2:3], param("lambda", 0), param("lambda", 1), ALU.mult).then_inc(ev["lam_prod"], 1))
            for k in range(0, KT, 2):
                dve.wait_ge(*ev.at("x_trans", k + 1))
                in_turn(v.tensor_copy(X[:, k, :], PSf[:, 0:NT]).then_inc(ev["x_moved0"], 1))
            dve.wait_ge(*ev.at("x_moved0", KT // 2))
            dve.wait_ge(*ev.at("x_moved1", KT // 2))
            in_turn(v.tensor_copy(small[:, 62:63], param("lambda", 0)).then_inc(ev["x_done"], 1))

            def norm(n, split_h=True):
                name = ("ffn1_norm", "mix_norm", "ffn2_norm", "final_norm")[n]
                dve.wait_ge(*ev.at("sq_used", (n + 1) * KT))
                in_turn(v.tensor_scalar(ch3(rstd), dense[0], 1.0 / D, EPS, ALU.mult, ALU.add).then_inc(ev["mean_made"], 1))
                dve.wait_ge(*ev.at("root_made", n + 1))
                in_turn(v.reciprocal(rstd, rstd))

                def low(k):
                    dve.wait_ge(*ev.at("h_high", n * KT + k + 1))
                    in_turn(v.tensor_tensor(H[1][:, k, :], T[:, k % 2, :], H[0][:, k, :].bitcast(F32), ALU.subtract)\
                        .then_inc(ev["h_ready"], 1))
                for k in range(KT):
                    dst = T[:, k % 2, :] if split_h else X[:, k, :]
                    in_turn(v.scalar_tensor_tensor(dst, X[:, k, :], param(name, k), rstd, ALU.mult, ALU.mult)\
                        .then_inc(ev["h_full"], 1))
                    if split_h and k:
                        low(k - 1)
                if split_h:
                    low(KT - 1)

            def ffn(first, pairs, last):
                for gi, (j0, n) in enumerate(GROUPS):
                    def up(i, end):
                        c = i + first
                        split(1, c)
                        split(0, c + 1)
                        dve.wait_ge(*ev.at("psum_free0", c + 1))
                        dve.wait_ge(*ev.at("unit_done1", c + 1))
                        in_turn(v.tensor_tensor(ch3(T[:, 1, :]), ch3(T[:, 0, :]), dense[1], ALU.mult)\
                            .then_inc(ev["ff_full"], 1))
                        dve.wait_ge(*ev.at("ff_high", i + (pairs + 1)))
                        in_turn(v.tensor_tensor(flat(G[1][:, ds(i, 1), :]), T[:, 1, :],
                                        flat(G[0][:, ds(i, 1), :]).bitcast(F32), ALU.subtract)\
                            .then_inc(ev["psum_free1"], 1))
                    loop(dve, n, up, False)
                    first += n
                    pairs += n

                    def down(i, end):
                        for s in range(2):
                            if s == 0 or not end:
                                split(1 - s, i + (first + s))
                            dve.wait_ge(*ev.at(f"unit_done{s}", i + (first + 1)))
                            xm = flat(X[:, ds(i * 2 + s, 1), :])
                            in_turn(v.scalar_tensor_tensor(ch3(xm), dense[s], 0.5, ch3(xm), ALU.mult, ALU.add)\
                                .then_inc(ev[f"psum_free{s}"], 1))
                    loop(dve, KT // 2, down, last and gi == len(GROUPS) - 1)
                    first += KT // 2
                dve.wait_ge(*ev.at("psum_free0", first))
                dve.wait_ge(*ev.at("psum_free1", first))
                in_turn(v.tensor_copy(small[:, 62:63], param("lambda", 0)).then_inc(ev["x_done"], 1))

            split(0, 0)
            norm(0)
            ffn(0, 0, False)
            norm(1)

            dve.wait_ge(*ev.at("rotary_loaded", 16))
            dve.wait_ge(*ev.at("x_saved", 16))

            def qk(dst, pair):
                def rope(i, end):
                    for s in range(2):
                        split(1 - s, i + (AT_QK + pair + s))
                        dve.wait_ge(*ev.at(f"unit_done{s}", i + (AT_QK + pair + 1)))
                        for b in range(4):
                            src, to = slice(32 * b, 32 * b + 32), slice(32 * (b ^ 1), 32 * (b ^ 1) + 32)
                            in_turn(v.tensor_tensor(ch3(T[to, s, :]), dense[s][src], ch3(rot[src, 1, :]), ALU.mult))
                        o = flat(dst[:, ds(i * 2 + s, 1), :])
                        in_turn(v.tensor_tensor(ch3(o), dense[s], ch3(rot[:, 0, :]), ALU.mult).then_inc(ev[f"psum_free{s}"], 1))
                        dve.wait_ge(*ev.at(f"psum_free{s}", i + (AT_QK + pair + 1)))
                        in_turn(v.tensor_tensor(o, o, T[:, s, :], ALU.add).then_inc(ev["rope_done"], 1))
                loop(dve, HP // 2, rope, False)
            qk(Q, 0)
            qk(Kr, HP // 2)

            def values(i, end):
                split(1, i + AT_V)
                split(0, i + (AT_V + 1))
            loop(dve, HP // 2, values, False)

            dve.wait_ge(*ev.at("rope_done", 2 * HP))
            dve.wait_ge(*ev.at("psum_free0", AT_GATES))
            dve.wait_ge(*ev.at("psum_free1", AT_GATES))
            in_turn(v.tensor_copy(vsam, Vt[:, :, NP:NT]))
            qk3 = qk_cols.rearrange("p (h b) -> p h b", b=NS)
            in_turn(v.tensor_tensor(qk3, Q[:, :, NP:NT], Kr[:, :, NP:NT], ALU.mult).then_inc(ev["s_self_prod"], 1))
            dve.wait_ge(*ev.at("s_self", 1))
            for a in range(2):
                in_turn(v.tensor_copy(sself.rearrange("p (b h a) -> p a h b", h=HP, a=2)[:, a],
                              PS[:, 7, 32 * a:32 * a + 32].rearrange("p (h b) -> p h b", b=NS)).then_inc(ev["s_self_moved"], 1))

            def gates(i, end):
                in_turn(v.tensor_tensor(Qdg.rearrange("p (h n) -> p h n", h=HP), over_heads(K("ident")),
                                bc(Q[:, :, ds(i + NP, 1)], P), ALU.mult).then_inc(ev["q_diag"], 1))
                split(1, i + AT_GATES)
                if not end:
                    split(0, i + (AT_GATES + 1))
                dve.wait_ge(*ev.at("q_bc", i + 1))
                for g in range(4):
                    dve.wait_ge(*ev.at(f"key_pages{g}", i * 64 + 64))
                    in_turn(v.tensor_tensor(prod.rearrange("p (j n) -> p j n", j=4), kring[:, g],
                                    Qbc.unsqueeze(1).broadcast_to([P, 4, 512]), ALU.mult).then_inc(ev[f"k_used{g}"], 1))
                    dve.wait_ge(*ev.at(f"k_used{g}", i + 1))
                    in_turn(v.tensor_reduce(SC[:, ds(i * 128 + 32 * g, 32)], prod.rearrange("p (a d) -> p a d", d=64), AX,
                                    ALU.add))
            loop(dve, GT // 2, gates, True)
            smx = smaxp.rearrange("p (b m) -> p b m", b=NS)
            in_turn(v.tensor_reduce(smx, SC.rearrange("p (b g m) -> p b m g", b=NS, g=PAGES), AX, ALU.max)\
                .then_inc(ev["s_max_part"], 1))

            dve.wait_ge(*ev.at("lam_exp", 1))
            in_turn(v.scalar_tensor_tensor(small[:, 3:4], small[:, 0:1], LAM_INIT, small[:, 1:2], ALU.add, ALU.subtract))
            for t in range(9):
                n = P if t < 8 else NS
                dve.wait_ge(*ev.at("v_trans", t + 1))
                dst = Vtok[:, t, :] if t < 8 else wT[1][:, 0:512]
                in_turn(v.tensor_copy(dst[0:n, :], PS[0:n, t % 2, :]).then_inc(ev["v_tok_made"], 1))

            dve.wait_ge(*ev.at("s_max_all", 1))
            dve.wait_ge(*ev.at("s_self_moved", 2))
            in_turn(v.tensor_tensor(smax, smax, sself, ALU.max))

            def pages(a):
                return a.rearrange("p (b m) -> p b m", b=NS).unsqueeze(2).broadcast_to([P, NS, PAGES, 2 * HP])
            in_turn(v.tensor_tensor(VIEW_SC, VIEW_SC, pages(smax), ALU.subtract).then_inc(ev["s_shifted"], 1))
            in_turn(v.tensor_tensor(sself, sself, smax, ALU.subtract).then_inc(ev["s_shifted"], 1))
            dve.wait_ge(*ev.at("s_exp", 2))
            in_turn(v.tensor_reduce(smx, SC.rearrange("p (b g m) -> p b m g", b=NS, g=PAGES), AX, ALU.add)\
                .then_inc(ev["s_sum_part"], 1))
            dve.wait_ge(*ev.at("s_sum", 1))
            in_turn(v.tensor_tensor(ssum, sexp, PS[:, 7, 0:64], ALU.add))
            in_turn(v.reciprocal(ssum, ssum))
            odd = ssum.rearrange("p (n a) -> p a n", a=2)[:, 1]
            in_turn(v.tensor_scalar(odd, odd, small[:, 3:4], None, ALU.mult))
            in_turn(v.tensor_tensor(VIEW_SC, VIEW_SC, pages(ssum), ALU.mult))
            in_turn(v.tensor_tensor(sexp, sexp, ssum, ALU.mult))
            two = SC.rearrange("p (n a) -> p a n", a=2)
            in_turn(v.tensor_tensor(Wp, two[:, 0], two[:, 1], ALU.subtract).then_inc(ev["s_weights"], 1))
            two = sexp.rearrange("p (n a) -> p a n", a=2)
            in_turn(v.tensor_tensor(wself, two[:, 0], two[:, 1], ALU.subtract).then_inc(ev["s_weights"], 1))
            dve.wait_ge(*ev.at("s_weights", 2))

            def sample_out(b):
                in_turn(v.tensor_tensor(vw.unsqueeze(2), vsam[:, :, b:b + 1],
                                wself.rearrange("p (b h) -> p h b", b=NS)[:, :, b:b + 1], ALU.mult))
                dve.wait_ge(*ev.at("osum_trans", b + 1))
                in_turn(v.tensor_tensor(Q[:, :, NP + b:NP + b + 1], PS[:, 7, 0:HP].unsqueeze(2), vw.unsqueeze(2), ALU.add)\
                    .then_inc(ev["o_sample"], 1))

            def maxima(step):
                qi, s = step // HP, step % 2
                n = (qi + 1) * P
                scores = PSf[:, 0:2048].rearrange("p (m n) -> p m n", m=2)
                dve.wait_ge(*ev.at("scores_done", step + 1))
                diag = scores[:, :, qi * P:n]
                in_turn(v.tensor_tensor(diag, diag, K("causal").unsqueeze(1).broadcast_to([P, 2, P]), ALU.add))
                top = small[:, 24 + 2 * s:26 + 2 * s]
                in_turn(v.tensor_reduce(top, scores[:, :, 0:n], AX, ALU.max))
                in_turn(v.tensor_scalar(small[:, 16 + 4 * s:18 + 4 * s], top, -SCALE, None, ALU.mult).then_inc(ev["neg_max"], 1))
            maxima(0)
            for step in range(STEPS):
                qi, s = step // HP, step % 2
                n = (qi + 1) * P
                dve.wait_ge(*ev.at("probs_made", 2 * step + 2))
                inv = small[:, 28 + 2 * s:30 + 2 * s]
                in_turn(v.reciprocal(inv, small[:, 18 + 4 * s:20 + 4 * s]))
                in_turn(v.tensor_tensor(inv[:, 1:2], inv[:, 1:2], small[:, 3:4], ALU.mult))
                p2 = pr[:, s, 1, 0:n]
                in_turn(v.tensor_scalar(p2, p2, inv[:, 1:2], None, ALU.mult))
                p1 = pr[:, s, 0, 0:n]
                in_turn(v.scalar_tensor_tensor(p1, p1, inv[:, 0:1], p2, ALU.mult, ALU.subtract).then_inc(ev["w_ready"], 1))
                if qi >= 4:
                    dve.wait_ge(*ev.at("w_trans_hi", step + 1 - 4 * HP))
                    in_turn(v.tensor_copy(wT[s][:, 512:n], PS[:, 5, 0:n - 512]).then_inc(ev["w_hi_moved"], 1))
                if step + 1 < STEPS:
                    maxima(step + 1)
                for b in range(NS):
                    if FILL_STEP[4 * b + 3] == step - 1:
                        sample_out(b)
            sample_out(NS - 1)

            for h in range(HP):
                dve.wait_ge(*ev.at("o_sq_sum", h + 1))
                in_turn(v.tensor_scalar(ch3(rstd), dense[0], 1.0 / P, EPS, ALU.mult, ALU.add).then_inc(ev["o_mean"], 1))
                dve.wait_ge(*ev.at("o_root", h + 1))
                in_turn(v.reciprocal(rstd, rstd))
                in_turn(v.scalar_tensor_tensor(Q[:, h, :], Q[:, h, :], param("da_subln", h), rstd, ALU.mult, ALU.mult)\
                    .then_inc(ev["yb_done"], 1))

            split(0, AT_Z)

            def z_mix(i, end):
                for s in range(2):
                    if s == 0 or not end:
                        split(1 - s, i + (AT_Z + s))
                    m = i * 2 + s
                    dve.wait_ge(*ev.at(f"psum_free{s}", i + (AT_Z + 1)))
                    zm = flat(Z[:, ds(m, 1), :])
                    z = T[:, s, :]
                    in_turn(v.tensor_copy(zlast[:, :, ds(m, 1)], z[:, NP - 1:NT].unsqueeze(2)).then_inc(ev["z_last"], 1))
                    in_turn(v.tensor_tensor(zm[:, 1:NP], z[:, 0:NP - 1], z[:, 1:NP], ALU.subtract))
                    in_turn(v.tensor_scalar(zm[:, 0:1], z[:, 0:1], -1.0, None, ALU.mult))
                    in_turn(v.tensor_tensor(zm[:, NP:NT], zshift[:, :, ds(m, 1)].rearrange("p b a -> p (b a)"), z[:, NP:NT],
                                    ALU.subtract))
                    in_turn(v.scalar_tensor_tensor(zm, zm, par[:, ds(m + ROW["rw_mu"], 1)], z, ALU.mult, ALU.add)\
                        .then_inc(ev[f"z_mixed{s}"], 1))
            loop(dve, ZT // 2, z_mix, True)
            dve.wait_ge(*ev.at("z_rows_trans", 1))
            in_turn(v.tensor_copy(zrow[0:9 * ZT, :], PS[0:9 * ZT, 7, 0:P]).then_inc(ev["z_rows_made"], 1))
            dve.wait_ge(*ev.at("z_mixed0", ZT // 2))
            dve.wait_ge(*ev.at("z_mixed1", ZT // 2))
            dve.wait_ge(*ev.at("lora_loaded", 48))

            for h in range(HP):
                dve.wait_ge(*ev.at("pre_done", h))
                in_turn(v.tensor_scalar(KKn[:, h, :], Kf[:, h, :], param("rw_k_k", h), None, ALU.mult).then_inc(ev["kk_scaled"], 1))
                dve.wait_ge(*ev.at("lora_act", 2 * h + 2))
                ld = T[:, 0, :]
                in_turn(v.tensor_scalar(ld, ld, LOGDECAY, None, ALU.mult).then_inc(ev["ld_made"], 1))
                dve.wait_ge(*ev.at("ld_made", h + 1))
                in_turn(v.tensor_tensor_scan(CUM[:, h, 0:NP], fresh, ld[:, 0:NP], 0.0, ALU.mult, ALU.add))
                dve.wait_ge(*ev.at("kk_norm", h + 1))
                dve.wait_ge(*ev.at("kk_scaled", h + 1))
                nrm = T[:, 1, :]
                in_turn(v.tensor_scalar(nrm, nrm, 1e-12, None, ALU.max))
                in_turn(v.reciprocal(nrm, nrm))
                in_turn(v.tensor_tensor(KKn[:, h, :], KKn[:, h, :], nrm, ALU.mult))
                in_turn(v.tensor_scalar(nrm, Bf[:, h, :], param("rw_k_a", h), small[:, 32 + h:33 + h], ALU.mult, ALU.add))
                in_turn(v.tensor_tensor(Kf[:, h, :], Kf[:, h, :], nrm, ALU.mult))
                in_turn(v.tensor_tensor(Bf[:, h, :], Bf[:, h, :], KKn[:, h, :], ALU.mult))
                dve.wait_ge(*ev.at("w_sample", h + 1))
                in_turn(v.tensor_copy(small[:, 62:63], param("lambda", 0)).then_inc(ev["pre_done"], 1))

            dve.wait_ge(*ev.at("z_stored", 32))
            for a in zeroed + [Ss]:
                in_turn(v.memset(a, 0.0))
            for x in range(2):
                in_turn(v.memset(Pb[x][:, :, 0:1], 1.0))
            in_turn(v.tensor_copy(small[:, 62:63], param("lambda", 0)).then_inc(ev["ck_zeroed"], 1))

            with dve.Fori(0, NC // 2) as i:
                lo, hi = halves
                for x in range(2):
                    now = ds(i * (2 * C) + x * C, C)
                    dve.wait_ge(*ev.at("ck_p", i * 4 + (2 * x + 2)))
                    in_turn(v.tensor_tensor(bts[x], Bf[:, :, now], Pinv[x], ALU.mult).then_inc(ev["ck_bt"], 1))
                    in_turn(v.scalar_tensor_tensor(ar[x][:, :, 0, :], KKn[:, :, now], -1.0, Pb[x][:, :, 0:64], ALU.mult, ALU.mult)\
                        .then_inc(ev["ck_at"], 1))
                    in_turn(v.tensor_tensor(ar[x][:, :, 1, :], Rf[:, :, now], Pb[x][:, :, 1:65], ALU.mult)\
                        .then_inc(ev["ck_rt"], 1))
                    for q in halves:
                        in_turn(v.tensor_tensor(ktd[x][q, :, q], Kf[q, :, now], Pinv[x][q], ALU.mult).then_inc(ev["ck_kt"], 1))
                strict, incl, eye = (over_heads(K(n)) for n in ("strict_st", "incl_st", "ident_stack"))
                for x in range(2):
                    dve.wait_ge(*ev.at("ck_gram", i * 2 + (x + 1)))
                    ab = AB_PS[x]
                    in_turn(v.tensor_tensor(LTs[x], ab[:, :, 0:64], strict, ALU.mult).then_inc(ev["ck_lt"], 1))
                    in_turn(v.tensor_tensor(Xs[x], T1_PS[x], over_heads(K("pair_ts")), ALU.mult))
                    in_turn(v.tensor_tensor(Xs[x], Xs[x], eye, ALU.add).then_inc(ev["ck_x"], 1))
                    in_turn(v.tensor_tensor(Ys[x], LTs[x], over_heads(K("pair_st")), ALU.mult))
                    in_turn(v.tensor_tensor(Ys[x], Ys[x], eye, ALU.add))
                    for q in halves:
                        in_turn(v.tensor_copy(Yd[x][q, :, q], Ys[x][q]).then_inc(ev["ck_yd_first"], 1))
                for x in range(2):
                    ab, ak = AB_PS[x], AK_PS[x]
                    for q in halves:
                        in_turn(v.tensor_tensor(aakd[x][q, :, q], ak[q, :, 0:64], strict[q], ALU.mult))
                    in_turn(v.tensor_tensor(arks[x], ak[:, :, 64:128], incl, ALU.mult))
                    in_turn(v.tensor_tensor(arbs[x], ab[:, :, 64:128], incl, ALU.mult).then_inc(ev["ck_ar"], 1))
                for l in range(LEVELS):
                    for x in range(2):
                        dve.wait_ge(*ev.at("ck_t1", level(i, l, x)))
                        if l < LEVELS - 1:
                            in_turn(v.tensor_copy(T1s[x][lo], T1_PS[x][lo]))
                        in_turn(v.tensor_copy(T1d[x][lo, :, lo], T1_PS[x][lo]).then_inc(ev["ck_t1_dve"], 1))
                    for x in range(2):
                        dve.wait_ge(*ev.at("ck_d", level(i, l, x)))
                        if l < LEVELS - 1:
                            in_turn(v.tensor_tensor(Xs[x], Xs[x], D_PS[x][:, 0:HP], ALU.add).then_inc(ev["ck_xs"], 1))
                        in_turn(v.tensor_tensor(Ys[x], Ys[x], D_PS[x][:, HP:2 * HP], ALU.add).then_inc(ev["ck_ys"], 1))
                        in_turn(v.tensor_copy(Yd[x][lo, :, lo], Ys[x][lo]).then_inc(ev["ck_yd_dve"], 1))
                for x in range(2):
                    dve.wait_ge(*ev.at("ck_u", i * 2 + (x + 1)))
                    in_turn(v.tensor_copy(Us[lo], U_PS[lo]))
                    in_turn(v.tensor_copy(Ud[lo, :, lo], U_PS[lo]).then_inc(ev["ck_u_dve"], 1))
                    dve.wait_ge(*ev.at("ck_ds", i * 2 + (x + 1)))
                    in_turn(v.tensor_tensor(Ss, Ss, DS_PS, ALU.add))
                    in_turn(v.tensor_tensor(Ss, Ss, bc(Pb[x][:, :, 64:65], 64), ALU.mult).then_inc(ev["ck_s"], 1))
                    in_turn(v.tensor_copy(Sd[1 - x][lo, :, lo], Ss[lo]))
                    in_turn(v.tensor_copy(Sd[1 - x][hi, :, hi], Ss[hi]).then_inc(ev["ck_state"], 1))

            dve.wait_ge(*ev.at("wkv_trans", 1))
            for q in halves:
                in_turn(v.tensor_copy(wfin[q], ps4(0, 0, 128)[q, :, q]).then_inc(ev["wkv_made"], 1))

            dve.wait_ge(*ev.at("state_loaded", 16 * NS))
            for h in range(HP):
                for n, vec in enumerate((KKn[:, h, NP:NT], wsam[:, h, :], Bf[:, h, NP:NT], Kf[:, h, NP:NT], Rf[:, h, NP:NT])):
                    in_turn(v.tensor_tensor(dg[:, n], K("ident_stack").unsqueeze(1).broadcast_to([P, NS, 64]),
                                    vec.unsqueeze(2).broadcast_to([P, NS, 64]), ALU.mult).then_inc(ev["row_diag"], 1))
                dve.wait_ge(*ev.at("rows_made", h + 1))
                row = [PS[:, n, :].rearrange("p (b j) -> p b j", b=NS) for n in range(5)]
                S = St[:, h]
                in_turn(v.tensor_tensor(stm, S, row[0], ALU.mult))
                in_turn(v.tensor_reduce(sa, stm, AX, ALU.add))
                in_turn(v.tensor_tensor(S, S, row[1], ALU.mult))
                in_turn(v.tensor_tensor(stm, sa.unsqueeze(2).broadcast_to([P, NS, 64]), row[2], ALU.mult))
                in_turn(v.tensor_tensor(S, S, stm, ALU.subtract))
                in_turn(v.tensor_tensor(stm, Vf[:, h, NP:NT].unsqueeze(2).broadcast_to([P, NS, 64]), row[3], ALU.mult))
                in_turn(v.tensor_tensor(S, S, stm, ALU.add))
                in_turn(v.tensor_tensor(stm, S, row[4], ALU.mult))
                in_turn(v.tensor_reduce(CUM[:, h, NP:NT], stm, AX, ALU.add))
                in_turn(v.tensor_copy(small[:, 62:63], param("lambda", 0)).then_inc(ev["state_new"], 1))

            for h in range(HP):
                y, t0, t1 = CUM[:, h, :], T[:, 0, :], T[:, 1, :]
                dve.wait_ge(*ev.at("y_sum", h + 1))
                dve.wait_ge(*ev.at("ya_high", h))
                in_turn(v.scalar_tensor_tensor(ch3(t0), dense[0], -1.0 / 64, ch3(y), ALU.mult, ALU.add).then_inc(ev["y_centred"], 1))
                dve.wait_ge(*ev.at("y_sq_sum", h + 1))
                in_turn(v.tensor_scalar(ch3(rstd), dense[1], 1.0 / 64, GN_EPS, ALU.mult, ALU.add).then_inc(ev["y_var"], 1))
                in_turn(v.scalar_tensor_tensor(t1, Rf[:, h, :], param("rw_r_k", h), Kf[:, h, :], ALU.mult, ALU.mult)\
                    .then_inc(ev["bonus_prod"], 1))
                dve.wait_ge(*ev.at("y_root", h + 1))
                in_turn(v.reciprocal(rstd, rstd))
                in_turn(v.scalar_tensor_tensor(t0, t0, param("rw_ln_w", h), rstd, ALU.mult, ALU.mult))
                dve.wait_ge(*ev.at("bonus_sum", h + 1))
                in_turn(v.tensor_tensor(ch3(t1), ch3(Vf[:, h, :]), dense[0], ALU.mult))
                in_turn(v.scalar_tensor_tensor(t0, t0, param("rw_ln_b", h), t1, ALU.add, ALU.add))
                dve.wait_ge(*ev.at("g_made", h + 1))
                in_turn(v.tensor_tensor(ch3(t0), ch3(t0), dense[1], ALU.mult).then_inc(ev["y_final"], 1))
                dve.wait_ge(*ev.at("ya_high", h + 1))
                in_turn(v.tensor_tensor(YA[1][:, h, :], t0, YA[0][:, h, :].bitcast(F32), ALU.subtract).then_inc(ev["ya_split"], 1))
                in_turn(v.tensor_copy(small[:, 62:63], param("lambda", 0)))
                in_turn(v.tensor_copy(small[:, 63:64], param("lambda", 0)))
            for h in range(HP):
                dve.wait_ge(*ev.at("yb_high", h + 1))
                in_turn(v.tensor_tensor(YB[1][:, h, :], Q[:, h, :], YB[0][:, h, :].bitcast(F32), ALU.subtract)\
                    .then_inc(ev["yb_split"], 1))

            split(0, AT_MERGE)

            def merge(i, end):
                for s in range(2):
                    split(1 - s, i + (AT_MERGE + s))
                    dve.wait_ge(*ev.at(f"unit_done{s}", i + (AT_MERGE + 1)))
                    dve.wait_ge(*ev.at(f"gates_back{s}", i * 32 + 32))
                    m = i * 2 + s
                    ga, gb = gring[:, s, 0, :], gring[:, s, 1, :]
                    dve.wait_ge(*ev.at("merge_high", m))
                    in_turn(v.tensor_tensor(ch3(T[:, 0, :]), ch3(ga), dense[0], ALU.mult))
                    in_turn(v.tensor_tensor(ch3(T[:, 1, :]), ch3(gb), dense[1], ALU.mult).then_inc(ev[f"psum_free{s}"], 1))
                    dve.wait_ge(*ev.at(f"psum_free{s}", i + (AT_MERGE + 1)))
                    in_turn(v.tensor_tensor(T[:, 0, :], T[:, 0, :], T[:, 1, :], ALU.add).then_inc(ev["merge_full"], 1))
                    dve.wait_ge(*ev.at("merge_high", m + 1))
                    in_turn(v.tensor_tensor(flat(M[1][:, ds(m, 1), :]), T[:, 0, :], flat(M[0][:, ds(m, 1), :]).bitcast(F32),
                                    ALU.subtract).then_inc(ev["merged"], 1))
            loop(dve, KT // 2, merge, False)
            dve.wait_ge(*ev.at("x_back", 16))

            def out(i, end):
                for s in range(2):
                    split(1 - s, i + (AT_OUT + s))
                    dve.wait_ge(*ev.at(f"unit_done{s}", i + (AT_OUT + 1)))
                    xm = flat(X[:, ds(i * 2 + s, 1), :])
                    in_turn(v.tensor_tensor(ch3(xm), ch3(xm), dense[s], ALU.add).then_inc(ev[f"psum_free{s}"], 1))
            loop(dve, KT // 2, out, False)
            dve.wait_ge(*ev.at("psum_free0", AT_FFN2))
            dve.wait_ge(*ev.at("psum_free1", AT_FFN2))
            in_turn(v.tensor_copy(small[:, 62:63], param("lambda", 0)).then_inc(ev["x_done"], 1))
            norm(2)
            ffn(AT_FFN2, FT, True)
            norm(3, False)
            for t in range(0, 9, 2):
                n = P if t < 8 else NS
                dve.wait_ge(*ev.at("y_trans", t + 1))
                if t >= 2:
                    dve.wait_ge(*ev.at("y_stored0", 16 * (t // 2)))
                in_turn(v.tensor_copy(yout[0][0:n, :], PSf[0:n, 0:1024]).then_inc(ev["y_moved0"], 1))

        @block.tensor
        def _(pe):
            ev.prime(pe, "tensor")
            mm = nc.tensor.matmul

            def product(s, R, nk, k0=0, w0=0, ready=None):
                for k in range(nk):
                    if ready is not None:
                        pe.wait_ge(*ev.at("h_ready", ready + k + 1))
                    for n, (w, r) in enumerate(((whi, R[0]), (whi, R[1]), (wlo, R[0]))):
                        for j in range(NCH):
                            last = mm(dense[s][:, j], w[w0][:, k0 + k, :], r[:, k, j * CH:(j + 1) * CH],
                                      start=(k == 0 and n == 0), stop=(k == nk - 1 and n == 2))
                return last

            def unit(s, c, R, nk=KT, ready=None):
                pe.wait_ge(*ev.at(f"w_split{s}", c + 1))
                pe.wait_ge(*ev.at(f"psum_free{s}", c))
                product(s, R, nk, 0, s, ready).then_inc(ev[f"unit_done{s}"], 1)

            def column_sums(s, what, src):
                for j in range(NCH):
                    last = mm(dense[s][:, j], what, src[:, j * CH:(j + 1) * CH], start=True, stop=True)
                return last

            pe.wait_ge(*ev.at("params_loaded", 16 * (len(PARAMS) + 6)))
            nc.tensor.transpose(PS[:, 7, 0:NROWS], prow[0:NROWS, :], K("ident")[0:NROWS, 0:NROWS])
            nc.tensor.transpose(PS[:, 7, P:P + NS * ZT], srow[0:NS * ZT, :], K("ident")[0:NS * ZT, 0:NS * ZT])\
                .then_inc(ev["par_trans"], 1)
            pe.wait_ge(*ev.at("x_loaded", 16 * 9))
            for k in range(KT):
                base = 1536 * (k % 2)
                if k >= 2:
                    pe.wait_ge(*ev.at(f"x_moved{k % 2}", k // 2))
                for t in range(8):
                    nc.tensor.transpose(PSf[:, base + t * P:base + (t + 1) * P], xin[:, t, k * P:(k + 1) * P], K("ident"))
                nc.tensor.transpose(PSf[:, base + NP:base + NT], xin[0:NS, 8, k * P:(k + 1) * P], K("ident")[0:NS, 0:NS])\
                    .then_inc(ev["x_trans"], 1)

            def norm(n):
                for k in range(KT):
                    pe.wait_ge(*ev.at("sq_made", n * KT + k + 1))
                    for j in range(NCH):
                        last = mm(dense[0][:, j], K("ones"), T[:, k % 2, j * CH:(j + 1) * CH],
                                  start=(k == 0), stop=(k == KT - 1))
                    last.then_inc(ev["sq_used"], 1)

            def ffn(first, ready):
                for gi, (j0, n) in enumerate(GROUPS):
                    if gi == 0:
                        unit(0, first, H, ready=ready)
                        unit(1, first, H)
                    with pe.Fori(1 if gi == 0 else 0, n) as i:
                        for s in range(2):
                            unit(s, i + first, H)
                    first += n
                    pe.wait_ge(*ev.at("psum_free1", first))

                    def down(i, end):
                        for s in range(2):
                            unit(s, i + first, G, n)
                    loop(pe, KT // 2, down)
                    first += KT // 2

            norm(0)
            ffn(0, 0)
            norm(1)

            def units(first, n, R):
                def body(i, end):
                    for s in range(2):
                        unit(s, i + first, R)
                loop(pe, n // 2, body)
            unit(0, AT_QK, H, ready=KT)
            unit(1, AT_QK, H)
            units(AT_QK + 1, 3 * HP - 2, H)

            pe.wait_ge(*ev.at("s_self_prod", 1))
            mm(PS[:, 7, 0:32], K("top_ones"), qk_cols, start=True, stop=True)
            mm(PS[:, 7, 32:64], K("bottom_ones"), qk_cols, start=True, stop=True).then_inc(ev["s_self"], 1)

            def gates(i, end):
                unit(0, i + AT_GATES, H)
                pe.wait_ge(*ev.at("q_diag", i + 1))
                pe.wait_ge(*ev.at("q_bc", i))
                mm(PS[:, 6, :], K("ones"), Qdg, start=True, stop=True).then_inc(ev["q_rows"], 1)
                unit(1, i + AT_GATES, H)
            gates(0, False)
            with pe.Fori(1, GT // 2) as i:
                gates(i, False)
            pe.wait_ge(*ev.at("s_self_moved", 2))

            pe.wait_ge(*ev.at("lam_prod", 1))
            mm(PS[:, 7, 0:1], K("top_ones"), small[:, 2:3], start=True, stop=True)
            mm(PS[:, 7, 1:2], K("bottom_ones"), small[:, 2:3], start=True, stop=True).then_inc(ev["lam_sums"], 1)
            pe.wait_ge(*ev.at("psum_free0", AT_Z))
            pe.wait_ge(*ev.at("psum_free1", AT_Z))
            pe.wait_ge(*ev.at("rope_done", 2 * HP))
            for t in range(9):
                n = P if t < 8 else NS
                if t >= 2:
                    pe.wait_ge(*ev.at("v_tok_made", t - 1))
                    pe.wait_ge(*ev.at("k_tok_made", t - 1))
                for h in range(HP):
                    last = nc.tensor.transpose(PS[0:n, t % 2, h * P:(h + 1) * P], Vt[:, h, t * P:t * P + n], K("ident"))
                last.then_inc(ev["v_trans"], 1)
                for h in range(HP):
                    last = nc.tensor.transpose(PS[0:n, 2 + t % 2, h * P:(h + 1) * P], Kr[:, h, t * P:t * P + n], K("ident"))
                last.then_inc(ev["k_trans"], 1)

            pe.wait_ge(*ev.at("s_sum_part", 1))
            pe.wait_ge(*ev.at("lam_exp", 1))
            mm(PS[:, 7, 0:64], K("ones"), smaxp, start=True, stop=True).then_inc(ev["s_sum"], 1)
            pe.wait_ge(*ev.at("v_tok_made", 9))
            pe.wait_ge(*ev.at("k_tok_made", 9))

            def weight_values(f):
                b = f // 4
                pe.wait_ge(*ev.at(f"value_pages{f % 2}", 64 * (f // 2 + 1)))
                if f % 4 == 0:
                    pe.wait_ge(*ev.at("s_weights", 2))
                    if b:
                        pe.wait_ge(*ev.at("o_sample", b))
                for j in range(4):
                    g = 4 * (f % 4) + j
                    last = mm(PS[0:HP, 7, :], VIEW_W[:, b, g, :], vring[:, f % 2, j, :], start=(g == 0), stop=(g == PAGES - 1))
                last.then_inc(ev["value_used"], 1)

            def turn_sums(b):
                pe.wait_ge(*ev.at("osum_moved", b + 1))
                for h in range(HP):
                    last = mm(PS[:, 7, h:h + 1], osum[0:HP, h * P:(h + 1) * P], K("ident")[0:HP, h:h + 1], start=True, stop=True)
                last.then_inc(ev["osum_trans"], 1)

            def scores(step):
                qi, h = step // HP, step % HP
                n = (qi + 1) * P
                pe.wait_ge(*ev.at("probs_made", 2 * step))
                for m in range(2):
                    q = halves[m]
                    for j in range(0, n, 512):
                        w = min(512, n - j)
                        last = mm(PSf[:, m * 1024 + j:m * 1024 + j + w], Q[q, h, qi * P:n], Kr[q, h, j:j + w],
                                  start=True, stop=True)
                last.then_inc(ev["scores_done"], 1)
            scores(0)
            for step in range(8 * HP):
                qi, h, s = step // HP, step % HP, step % 2
                if step + 1 < 8 * HP:
                    scores(step + 1)
                pe.wait_ge(*ev.at("w_ready", step + 1))
                pe.wait_ge(*ev.at("w_lo_moved", step))
                for t in range(qi + 1):
                    if t == 4 and step > 4 * HP:
                        pe.wait_ge(*ev.at("w_hi_moved", step - 4 * HP))
                    last = nc.tensor.transpose(PS[:, 4 + t // 4, (t % 4) * P:(t % 4 + 1) * P],
                                               pr[:, s, 0, t * P:(t + 1) * P], K("ident"))
                    if t == min(3, qi):
                        last.then_inc(ev["w_trans_lo"], 1)
                    elif t == qi:
                        last.then_inc(ev["w_trans_hi"], 1)
                pe.wait_ge(*ev.at("w_lo_moved", step + 1))
                if qi >= 4:
                    pe.wait_ge(*ev.at("w_hi_moved", step + 1 - 4 * HP))
                if step:
                    pe.wait_ge(*ev.at("o_moved", step))
                for t in range(qi + 1):
                    last = mm(PS[:, 6, 0:P], Vtok[:, t, h * P:(h + 1) * P], wT[s][:, t * P:(t + 1) * P],
                              start=(t == 0), stop=(t == qi))
                last.then_inc(ev["o_done"], 1)
                for b in range(NS):
                    if FILL_STEP[4 * b + 3] == step - 1:
                        turn_sums(b)
                for f in range(4 * NS):
                    if FILL_STEP[f] == step:
                        weight_values(f)
            turn_sums(NS - 1)

            pe.wait_ge(*ev.at("o_sample", NS))
            for h in range(HP):
                pe.wait_ge(*ev.at("o_sq", h + 1))
                if h:
                    pe.wait_ge(*ev.at("o_mean", h))
                column_sums(0, K("ones"), T[:, h % 2, :]).then_inc(ev["o_sq_sum"], 1)
            pe.wait_ge(*ev.at("o_mean", HP))

            units(AT_Z, ZT, H)
            pe.wait_ge(*ev.at("z_last", ZT))
            nc.tensor.transpose(PS[0:9 * ZT, 7, 0:P], flat(zlast), K("ident")).then_inc(ev["z_rows_trans"], 1)
            pe.wait_ge(*ev.at("psum_free0", AT_MERGE))
            pe.wait_ge(*ev.at("psum_free1", AT_MERGE))
            pe.wait_ge(*ev.at("lora_loaded", 48))
            pe.wait_ge(*ev.at("z_act", 2))
            for h in range(HP):
                hh = slice(h * P, (h + 1) * P)
                if h:
                    pe.wait_ge(*ev.at("kk_norm", h))
                    pe.wait_ge(*ev.at("lora_act", 2 * h))
                for q, d in ((halves[0], 0), (halves[1], 1)):
                    for j in range(NCH):
                        last = mm(dense[d][:, j], lw2[q, hh], Z[q, 12, j * CH:(j + 1) * CH], start=True, stop=True)
                last.then_inc(ev["lora_made"], 1)
                pe.wait_ge(*ev.at("kk_sq", h + 1))
                pe.wait_ge(*ev.at("lora_act", 2 * h + 2))
                column_sums(0, K("block_ones"), T[:, 1, :]).then_inc(ev["kk_sum"], 1)
            pe.wait_ge(*ev.at("kk_norm", HP))
            pe.wait_ge(*ev.at("z_rows_made", 1))

            with pe.Fori(0, NC // 2) as i:
                pe.wait_ge(*ev.at("ck_y_out", i * 2))
                for x in range(2):
                    pe.wait_ge(*ev.at("ck_btd", i * 2 + (x + 1)))
                    pe.wait_ge(*ev.at("ck_kt", i * 4 + (2 * x + 2)))
                    pe.wait_ge(*ev.at("ck_atd", i * 2 + (x + 1)))
                    both = ar[x].rearrange("p h a t -> p h (a t)")
                    for h in range(HP):
                        mm(AB_PS[x][:, h], btd[x][:, h], both[:, h], start=True, stop=True)
                    for h in range(HP):
                        mm(T1_PS[x][:, h], atd[x][:, h], bts[x][:, h], start=True, stop=True)
                    for h in range(HP):
                        last = mm(AK_PS[x][:, h], ktd[x][:, h], both[:, h], start=True, stop=True)
                    last.then_inc(ev["ck_gram"], 1)

                def turn(k):
                    if k >= 2:
                        pe.wait_ge(*ev.at("ck_tok_moved", i * 8 + (k - 1)))
                    src = (vtd[0], vtd[0], vtd[1], vtd[1], btd[0], btd[1], ktd[0], ktd[1])[k]
                    for h in range(HP):
                        if k in (0, 2):
                            last = mm(TOKEN_MAJOR[k][1][:, h], src[:, h], K("ident_stack"), start=True, stop=True)
                        else:
                            last = nc.tensor.transpose(TOKEN_MAJOR[k][1][:, h], src[:, h], K("ident"))
                    last.then_inc(ev["ck_tok"], 1)
                pe.wait_ge(*ev.at("ck_vtd", i * 4 + 4))
                for k in range(4):
                    turn(k)
                for l in range(LEVELS):
                    for x in range(2):
                        pe.wait_ge(*ev.at("ck_mask", i * (4 * LEVELS) + (4 * l + 2 * x + 2)))
                        if l == 0:
                            pe.wait_ge(*ev.at("ck_x", i * 2 + (x + 1)))
                        else:
                            pe.wait_ge(*ev.at("ck_xs", i * (2 * LEVELS - 2) + (2 * l + x - 1)))
                        for h in range(HP):
                            last = mm(T1_PS[x][:, h], btmd[x][:, h], Xs[x][:, h], start=True, stop=True)
                        last.then_inc(ev["ck_t1"], 1)
                    if l < 2:
                        turn(4 + 2 * l)
                        turn(5 + 2 * l)
                    for x in range(2):
                        if l == 0:
                            pe.wait_ge(*ev.at("ck_yd_first", i * 4 + (2 * x + 2)))
                            pe.wait_ge(*ev.at("ck_ar", i * 2 + (x + 1)))
                        else:
                            pe.wait_ge(*ev.at("ck_yd_dve", level(i, l - 1, x)))
                            pe.wait_ge(*ev.at("ck_yd_act", level(i, l - 1, x)))
                        pe.wait_ge(*ev.at("ck_t1_act", level(i, l, x)))
                        pe.wait_ge(*ev.at("ck_t1_dve", level(i, l, x)))
                        if l < LEVELS - 1:
                            for h in range(HP):
                                mm(D_PS[x][:, h], Yd[x][:, h], T1s[x][:, h], start=True, stop=True)
                        for h in range(HP):
                            last = mm(D_PS[x][:, HP + h], T1d[x][:, h], Ys[x][:, h], start=True, stop=True)
                        last.then_inc(ev["ck_d"], 1)
                for x in range(2):
                    pe.wait_ge(*ev.at("ck_tok_moved", i * 8 + 8))
                    pe.wait_ge(*ev.at("ck_s", i * 2 + x))
                    for h in range(HP):
                        mm(R_PS[:, h], aakd[x][:, h], vts[x][:, h], start=True, stop=False)
                        last = mm(R_PS[:, h], atd[x][:, h], Ss[:, h], start=False, stop=True)
                    last.then_inc(ev["ck_r"], 1)
                    pe.wait_ge(*ev.at("ck_yd_dve", level(i, LEVELS - 1, x)))
                    pe.wait_ge(*ev.at("ck_yd_act", level(i, LEVELS - 1, x)))
                    pe.wait_ge(*ev.at("ck_r_moved", i * 2 + (x + 1)))
                    for h in range(HP):
                        last = mm(U_PS[:, h], Yd[x][:, h], Rs[:, h], start=True, stop=True)
                    last.then_inc(ev["ck_u"], 1)
                    pe.wait_ge(*ev.at("ck_u_act", i * 2 + (x + 1)))
                    pe.wait_ge(*ev.at("ck_u_dve", i * 2 + (x + 1)))
                    for h in range(HP):
                        mm(DS_PS[:, h], ktok[x][:, h], vts[x][:, h], start=True, stop=False)
                        last = mm(DS_PS[:, h], btok[x][:, h], Us[:, h], start=False, stop=True)
                    last.then_inc(ev["ck_ds"], 1)
                    pe.wait_ge(*ev.at("ck_state", i * 2 + x))
                    if x:
                        pe.wait_ge(*ev.at("ck_y_out", i * 2 + 1))
                    for h in range(HP):
                        mm(Y_PS[:, h], Sd[x][:, h], ar[x][:, h, 1, :], start=True, stop=False)
                        mm(Y_PS[:, h], Ud[:, h], arbs[x][:, h], start=False, stop=False)
                        last = mm(Y_PS[:, h], vtok[x][:, h], arks[x][:, h], start=False, stop=True)
                    last.then_inc(ev["ck_y"], 1)

            pe.wait_ge(*ev.at("ck_state", NC))
            for h in range(HP):
                last = nc.tensor.transpose(ps4(0, 0, 128)[:, h], Sd[0][:, h], K("ident"))
            last.then_inc(ev["wkv_trans"], 1)
            pe.wait_ge(*ev.at("wkv_made", 2))
            for h in range(HP):
                pe.wait_ge(*ev.at("row_diag", 5 * h + 5))
                if h:
                    pe.wait_ge(*ev.at("state_new", h))
                for n in range(5):
                    last = mm(PS[:, n, :], K("block_ones"), dg[:, n].rearrange("p b j -> p (b j)"), start=True, stop=True)
                last.then_inc(ev["rows_made"], 1)
            pe.wait_ge(*ev.at("state_new", HP))
            pe.wait_ge(*ev.at("g2_loaded", 16))
            pe.wait_ge(*ev.at("ck_y_out", NC))
            for h in range(HP):
                pe.wait_ge(*ev.at("y_final", h))
                column_sums(0, K("block_ones"), CUM[:, h, :]).then_inc(ev["y_sum"], 1)
                pe.wait_ge(*ev.at("y_sq", h + 1))
                column_sums(1, K("block_ones"), T[:, 1, :]).then_inc(ev["y_sq_sum"], 1)
                pe.wait_ge(*ev.at("bonus_prod", h + 1))
                column_sums(0, K("block_ones"), T[:, 1, :]).then_inc(ev["bonus_sum"], 1)
                column_sums(1, G2[:, h * P:(h + 1) * P], Z[:, 13, :]).then_inc(ev["g_made"], 1)
            pe.wait_ge(*ev.at("y_final", HP))

            pe.wait_ge(*ev.at("ya_split", HP))
            pe.wait_ge(*ev.at("yb_split", HP))

            def merge(i, end):
                for s in range(2):
                    pe.wait_ge(*ev.at(f"w_split{s}", i + (AT_MERGE + 1)))
                    pe.wait_ge(*ev.at(f"psum_free{s}", i + AT_MERGE))
                    pe.wait_ge(*ev.at(f"psum_free{1 - s}", i + (AT_MERGE + s)))
                    product(0, YA, HP, 0, s)
                    product(1, YB, HP, HP, s).then_inc(ev[f"unit_done{s}"], 1)
            loop(pe, KT // 2, merge)
            pe.wait_ge(*ev.at("merged", KT))
            pe.wait_ge(*ev.at("psum_free1", AT_OUT))
            units(AT_OUT, KT, M)
            norm(2)
            ffn(AT_FFN2, 2 * KT)
            norm(3)
            pe.wait_ge(*ev.at("h_full", 4 * KT))
            for t in range(9):
                n = P if t < 8 else NS
                if t >= 2:
                    pe.wait_ge(*ev.at(f"y_moved{t % 2}", t // 2))
                base = 1024 * (t % 2)
                for k in range(KT):
                    last = nc.tensor.transpose(PSf[0:n, base + k * P:base + (k + 1) * P], X[:, k, t * P:t * P + n], K("ident"))
                last.then_inc(ev["y_trans"], 1)


_INS = ["x_prompt", "x_sample", "cache_k", "cache_v", "state_wkv", "state_shift", "page_table",
        "ffn1_norm", "ffn1_up", "ffn1_down", "mix_norm", "w_in", "gate_bias",
        "rw_mu", "rw_w0", "rw_w2", "rw_a0", "rw_a2", "rw_g2", "rw_k_k", "rw_k_a", "rw_r_k", "rw_ln_w", "rw_ln_b",
        "da_lq1", "da_lk1", "da_lq2", "da_lk2", "da_subln", "w_proj_a", "w_proj_b", "w_out",
        "ffn2_norm", "ffn2_up", "ffn2_down", "final_norm"]
_OUTS = [("y_prompt", (1, NP, D)), ("y_sample", (NS, 1, D)),
         ("k_prompt", (1, 1, NP, 8, 64)), ("v_prompt", (1, 1, NP, 4, 128)),
         ("wkv_prompt", (1, 1, 8, 64, 64)), ("shift_prompt", (1, 1, RW_COLS)),
         ("k_sample", (1, NS, 1, 8, 64)), ("v_sample", (1, NS, 1, 4, 128)),
         ("wkv_sample", (1, NS, 8, 64, 64)), ("shift_sample", (1, NS, RW_COLS))]


def kernel(**inputs):
    import numpy as _np
    import concourse.bacc as _bacc
    from concourse import mybir as _mybir
    from concourse.bass_utils import run_bass_kernel_spmd as _run

    nc = _bacc.Bacc("TRN2", target_bir_lowering=False, num_devices=1)
    arrays, A = {}, {}
    for name in _INS:
        a = _np.ascontiguousarray(inputs[name])
        arrays["in_" + name] = a
        A[name] = nc.dram_tensor("in_" + name, a.shape, _mybir.dt.from_np(a.dtype), kind="ExternalInput").ap()
    for name, a in zip(("const_table", "const_rotary", "const_fresh"), shape_constants()):
        arrays[name] = _np.ascontiguousarray(a)
        A[name] = nc.dram_tensor(name, a.shape, F32, kind="ExternalInput").ap()
    for name, shape in _OUTS:
        A[name] = nc.dram_tensor("out_" + name, shape, F32, kind="ExternalOutput").ap()
    build(nc, A)
    r = _run(nc, [arrays], core_ids=[0])
    return tuple(r.results[0]["out_" + name] for name, _ in _OUTS)
```
